# Optimizing a Trainium2 kernel written in Bass

```python
import jax
import jax.numpy as jnp
from jax import lax
import numpy as np

D_MODEL = 2048
BATCH = 1
SEQ = 256
DEPTH = 1

CTX_LEN = 256
GRID_W = 64
EPS = 1e-6
N_MOD = 6

CONV_DIM = 2048
CONV_WIDTH = 31

DN_HEADS = 16
DN_DK = 128
DN_DV = 128
DN_QK = DN_HEADS * DN_DK
DN_V = DN_HEADS * DN_DV
SHORT_CONV = 5
CHUNK = 64

PEER_HEADS = 8
PEER_KEYS = 128
PEER_EXPERTS = PEER_KEYS * PEER_KEYS
PEER_QDIM = 256
PEER_HALF = PEER_QDIM // 2
PEER_TOPK = 16
PEER_BLOCK = 128

COL_GLU = 2 * CONV_DIM
COL_QKV = 2 * DN_QK + DN_V
COL_Z = DN_V
COL_AB = 4 * DN_HEADS
COL_BR = 2 * D_MODEL
IN_COLS = COL_GLU + COL_QKV + COL_Z + COL_AB + COL_BR


def rms_norm(x, g):
    xf = x.astype(jnp.float32)
    y = xf * lax.rsqrt(jnp.mean(xf * xf, axis=-1, keepdims=True) + EPS)
    return (y * g.astype(jnp.float32)).astype(x.dtype)

def layer_norm(x, g, b):
    xf = x.astype(jnp.float32)
    mu = jnp.mean(xf, axis=-1, keepdims=True)
    var = jnp.mean(jnp.square(xf - mu), axis=-1, keepdims=True)
    y = (xf - mu) * lax.rsqrt(var + EPS)
    return (y * g.astype(jnp.float32) + b.astype(jnp.float32)).astype(x.dtype)

def l2norm(x):
    xf = x.astype(jnp.float32)
    return xf * lax.rsqrt(jnp.sum(xf * xf, axis=-1, keepdims=True) + EPS)

def modulate(h, shift, scale):
    return h * (1.0 + scale[:, None, :]) + shift[:, None, :]

def dw_conv(x, w):
    pad = w.shape[0] // 2
    return lax.conv_general_dilated(x, w[:, None, :].astype(x.dtype), (1,), [(pad, pad)],
                                    dimension_numbers=('NWC', 'WIO', 'NWC'),
                                    feature_group_count=x.shape[-1])

def split_in_proj(p):
    s1 = COL_GLU
    s2 = s1 + COL_QKV
    s3 = s2 + COL_Z
    s4 = s3 + COL_AB
    return jnp.split(p, [s1, s2, s3, s4], axis=-1)

def conformer_conv(glu_in, conv_w, conv_b, ln_g, ln_b, w_conv_out, rows):
    a, gate = jnp.split(glu_in, 2, axis=-1)
    u = a * jax.nn.sigmoid(gate)
    B, L, C = u.shape
    if rows is not None:
        u = u.reshape(B * rows, GRID_W, C)
    u = (dw_conv(u, conv_w) + conv_b).reshape(B, L, C)
    u = jax.nn.silu(layer_norm(u, ln_g, ln_b))
    return u @ w_conv_out

def dn_qkv(qkv, short_w):
    B, L, _ = qkv.shape
    qkv = jax.nn.silu(dw_conv(qkv, short_w))
    q, k, v = jnp.split(qkv, [DN_QK, 2 * DN_QK], axis=-1)
    q = l2norm(q.reshape(B, L, DN_HEADS, DN_DK)) * (DN_DK ** -0.5)
    k = l2norm(k.reshape(B, L, DN_HEADS, DN_DK))
    v = v.reshape(B, L, DN_HEADS, DN_DV)
    return q, k, v

def dn_gates(ab, a_log, dt_bias):
    a, b = jnp.split(ab.astype(jnp.float32), 2, axis=-1)
    g = -jnp.exp(a_log.astype(jnp.float32)) * jax.nn.softplus(a + dt_bias.astype(jnp.float32))
    beta = jax.nn.sigmoid(b)
    return g, beta

def gated_delta_chunked(q, k, v, g, beta, s0):
    B, L, H, DK = q.shape
    DV = v.shape[-1]
    n = L // CHUNK

    def chunks(t):
        t = t.astype(jnp.float32).reshape((B, n, CHUNK) + t.shape[2:])
        return jnp.moveaxis(t, 1, 0).swapaxes(2, 3)

    qc, kc, vc, gc, bc = chunks(q), chunks(k), chunks(v), chunks(g), chunks(beta)
    gcum = jnp.cumsum(gc, axis=-1)
    tri = jnp.tril(jnp.ones((CHUNK, CHUNK), dtype=bool))
    strict = jnp.tril(jnp.ones((CHUNK, CHUNK), dtype=bool), -1)
    decay = jnp.exp(jnp.where(tri, gcum[..., :, None] - gcum[..., None, :], -jnp.inf))
    kb = kc * bc[..., None]
    m = jnp.where(strict, jnp.einsum('nbhik,nbhjk->nbhij', kb, kc) * decay, 0.0)
    eye = jnp.eye(CHUNK, dtype=jnp.float32)
    t_inv = lax.linalg.triangular_solve(m + eye, jnp.broadcast_to(eye, m.shape), left_side=True,
                                        lower=True, unit_diagonal=True)
    u = jnp.einsum('nbhij,nbhjv->nbhiv', t_inv, vc * bc[..., None])
    w = jnp.einsum('nbhij,nbhjk->nbhik', t_inv, kb * jnp.exp(gcum)[..., None])
    attn = jnp.einsum('nbhik,nbhjk->nbhij', qc, kc) * decay

    def step(S, inp):
        q_i, k_i, u_i, w_i, g_i, a_i = inp
        v_new = u_i - jnp.einsum('bhck,bhkv->bhcv', w_i, S)
        o = (jnp.einsum('bhck,bhkv->bhcv', q_i * jnp.exp(g_i)[..., None], S)
             + jnp.einsum('bhij,bhjv->bhiv', a_i, v_new))
        g_last = g_i[..., -1:]
        S = (S * jnp.exp(g_last)[..., None]
             + jnp.einsum('bhck,bhcv->bhkv', k_i * jnp.exp(g_last - g_i)[..., None], v_new))
        return S, o

    s_final, o = lax.scan(step, s0.astype(jnp.float32), (qc, kc, u, w, gcum, attn))
    o = jnp.moveaxis(o.swapaxes(2, 3), 0, 1).reshape(B, L, H, DV)
    return s_final, o

def bidirectional_deltanet(qkv_l, qkv_c, ab_l, ab_c, short_w, a_log, dt_bias):
    ql, kl, vl = dn_qkv(qkv_l, short_w)
    qc, kc, vc = dn_qkv(qkv_c, short_w)
    B = ql.shape[0]
    s0 = jnp.zeros((B, DN_HEADS, DN_DK, DN_DV), jnp.float32)
    o_l = jnp.zeros(vl.shape, jnp.float32)
    o_c = jnp.zeros(vc.shape, jnp.float32)
    for d in range(2):
        cols = slice(2 * d * DN_HEADS, (2 * d + 2) * DN_HEADS)
        gl, bl = dn_gates(ab_l[..., cols], a_log[d], dt_bias[d])
        gc, bc = dn_gates(ab_c[..., cols], a_log[d], dt_bias[d])
        seq_l = [ql, kl, vl, gl, bl]
        seq_c = [qc, kc, vc, gc, bc]
        if d == 1:
            seq_l = [jnp.flip(t, axis=1) for t in seq_l]
            seq_c = [jnp.flip(t, axis=1) for t in seq_c]
        s_ctx, oc = gated_delta_chunked(*seq_c, s0)
        _, ol = gated_delta_chunked(*seq_l, s_ctx)
        if d == 1:
            oc = jnp.flip(oc, axis=1)
            ol = jnp.flip(ol, axis=1)
        o_l = o_l + ol
        o_c = o_c + oc
    return o_l, o_c

def token_mixer(h, hc, w_in, conv_w, conv_b, conv_ln_g, conv_ln_b, w_conv_out, dn_short_w,
                dn_a_log, dn_dt_bias, dn_norm_g, w_dn_out, w_out, with_ctx_out):
    B, L, _ = h.shape
    rows = L // GRID_W
    glu_l, qkv_l, z_l, ab_l, br_l = split_in_proj(h @ w_in)
    glu_c, qkv_c, z_c, ab_c, br_c = split_in_proj(hc @ w_in)
    o_l, o_c = bidirectional_deltanet(qkv_l, qkv_c, ab_l, ab_c, dn_short_w, dn_a_log, dn_dt_bias)

    def merge(glu, z, br, o, rows_):
        Bq, Lq, _ = glu.shape
        y_conv = conformer_conv(glu, conv_w, conv_b, conv_ln_g, conv_ln_b, w_conv_out, rows_)
        o = rms_norm(o, dn_norm_g).astype(glu.dtype) * jax.nn.silu(z.reshape(Bq, Lq, DN_HEADS, DN_DV))
        y_dn = o.reshape(Bq, Lq, DN_V) @ w_dn_out
        g_conv, g_dn = jnp.split(jax.nn.sigmoid(br), 2, axis=-1)
        return (g_conv * y_conv + g_dn * y_dn) @ w_out

    y = merge(glu_l, z_l, br_l, o_l, rows)
    yc = merge(glu_c, z_c, br_c, o_c, None) if with_ctx_out else None
    return y, yc

def peer(h, w_q, key1, key2, u_tab, v_tab):
    B, L, D = h.shape
    T = B * L
    t = h.reshape(T, D)
    q = (t @ w_q).reshape(T, PEER_HEADS, PEER_QDIM).astype(jnp.float32)
    s1 = jnp.einsum('thd,hkd->thk', q[..., :PEER_HALF], key1.astype(jnp.float32))
    s2 = jnp.einsum('thd,hkd->thk', q[..., PEER_HALF:], key2.astype(jnp.float32))
    v1, i1 = lax.top_k(s1, PEER_TOPK)
    v2, i2 = lax.top_k(s2, PEER_TOPK)
    cand = (v1[..., :, None] + v2[..., None, :]).reshape(T, PEER_HEADS, PEER_TOPK * PEER_TOPK)
    cidx = (i1[..., :, None] * PEER_KEYS + i2[..., None, :]).reshape(T, PEER_HEADS, PEER_TOPK * PEER_TOPK)
    best, pos = lax.top_k(cand, PEER_TOPK)
    idx = jnp.take_along_axis(cidx, pos, axis=-1)
    wgt = jax.nn.softmax(best, axis=-1).astype(h.dtype)
    nb = T // PEER_BLOCK

    def expert_block(args):
        tb, ib, wb = args
        act = jax.nn.gelu(jnp.einsum('td,thkd->thk', tb, u_tab[ib]))
        return jnp.einsum('thk,thkd->td', wb * act, v_tab[ib])

    y = lax.map(expert_block, (t.reshape(nb, PEER_BLOCK, D),
                               idx.reshape(nb, PEER_BLOCK, PEER_HEADS, PEER_TOPK),
                               wgt.reshape(nb, PEER_BLOCK, PEER_HEADS, PEER_TOPK)))
    return y.reshape(B, L, D)

def first_inputs(seed: int = 0) -> dict:
    key = jax.random.key(seed)
    ks = jax.random.split(key, 28)
    f32 = jnp.float32
    D = D_MODEL

    def nrm(k, shape, scale):
        return jax.random.normal(k, shape, f32) * scale

    dt = jnp.exp(jax.random.uniform(ks[14], (DEPTH, 2, DN_HEADS), f32,
                                    float(np.log(1e-3)), float(np.log(1e-1))))
    return {
        'x': nrm(ks[0], (BATCH, SEQ, D), 1.0),
        'c': nrm(ks[1], (BATCH, D), 1.0),
        'ctx': nrm(ks[2], (BATCH, CTX_LEN, D), 1.0),
        'c_ctx': nrm(ks[3], (D,), 1.0),
        'w_mod': nrm(ks[4], (DEPTH, D, N_MOD * D), 0.5 * D ** -0.5),
        'b_mod': nrm(ks[5], (DEPTH, N_MOD * D), 0.02),
        'norm1_g': 1.0 + nrm(ks[6], (DEPTH, D), 0.05),
        'norm2_g': 1.0 + nrm(ks[7], (DEPTH, D), 0.05),
        'w_in': nrm(ks[8], (DEPTH, D, IN_COLS), D ** -0.5),
        'conv_w': nrm(ks[9], (DEPTH, CONV_WIDTH, CONV_DIM), CONV_WIDTH ** -0.5),
        'conv_b': nrm(ks[10], (DEPTH, CONV_DIM), 0.02),
        'conv_ln_g': 1.0 + nrm(ks[11], (DEPTH, CONV_DIM), 0.05),
        'conv_ln_b': nrm(ks[12], (DEPTH, CONV_DIM), 0.02),
        'w_conv_out': nrm(ks[13], (DEPTH, CONV_DIM, D), CONV_DIM ** -0.5),
        'dn_short_w': nrm(ks[15], (DEPTH, SHORT_CONV, COL_QKV), SHORT_CONV ** -0.5),
        'dn_a_log': jnp.log(jax.random.uniform(ks[16], (DEPTH, 2, DN_HEADS), f32, 1.0, 16.0)),
        'dn_dt_bias': dt + jnp.log(-jnp.expm1(-dt)),
        'dn_norm_g': 1.0 + nrm(ks[17], (DEPTH, DN_DV), 0.05),
        'w_dn_out': nrm(ks[18], (DEPTH, DN_V, D), DN_V ** -0.5),
        'w_out': nrm(ks[19], (DEPTH, D, D), D ** -0.5),
        'peer_w_q': nrm(ks[20], (DEPTH, D, PEER_HEADS * PEER_QDIM), D ** -0.5),
        'peer_key1': nrm(ks[21], (DEPTH, PEER_HEADS, PEER_KEYS, PEER_HALF), PEER_HALF ** -0.5),
        'peer_key2': nrm(ks[22], (DEPTH, PEER_HEADS, PEER_KEYS, PEER_HALF), PEER_HALF ** -0.5),
        'peer_u': nrm(ks[23], (DEPTH, PEER_EXPERTS, D), D ** -0.5),
        'peer_v': nrm(ks[24], (DEPTH, PEER_EXPERTS, D), PEER_HEADS ** -0.5),
        'final_g': 1.0 + nrm(ks[25], (D,), 0.05),
    }

def first_block(x, c, ctx, c_ctx, w_mod, b_mod, norm1_g, norm2_g, w_in, conv_w, conv_b, conv_ln_g,
              conv_ln_b, w_conv_out, dn_short_w, dn_a_log, dn_dt_bias, dn_norm_g, w_dn_out, w_out,
              peer_w_q, peer_key1, peer_key2, peer_u, peer_v, final_g):
    xc = ctx
    sc = jax.nn.silu(c)
    scc = jax.nn.silu(c_ctx)[None, :]
    for l in range(DEPTH):
        last = l == DEPTH - 1
        mod = jnp.split(sc @ w_mod[l] + b_mod[l], N_MOD, axis=-1)
        modc = jnp.split(scc @ w_mod[l] + b_mod[l], N_MOD, axis=-1)
        h = modulate(rms_norm(x, norm1_g[l]), mod[0], mod[1])
        hc = modulate(rms_norm(xc, norm1_g[l]), modc[0], modc[1])
        y, yc = token_mixer(h, hc, w_in[l], conv_w[l], conv_b[l], conv_ln_g[l], conv_ln_b[l],
                            w_conv_out[l], dn_short_w[l], dn_a_log[l], dn_dt_bias[l], dn_norm_g[l],
                            w_dn_out[l], w_out[l], not last)
        x = x + mod[2][:, None, :] * y
        h = modulate(rms_norm(x, norm2_g[l]), mod[3], mod[4])
        x = x + mod[5][:, None, :] * peer(h, peer_w_q[l], peer_key1[l], peer_key2[l], peer_u[l], peer_v[l])
        if not last:
            xc = xc + modc[2][:, None, :] * yc
            hc = modulate(rms_norm(xc, norm2_g[l]), modc[3], modc[4])
            xc = xc + modc[5][:, None, :] * peer(hc, peer_w_q[l], peer_key1[l], peer_key2[l],
                                                 peer_u[l], peer_v[l])
    return rms_norm(x, final_g)


BRANCH_WIDTH = 1024
N_BRANCH = 3
A_HEADS = 8
A_KEY = 128
A_VAL = BRANCH_WIDTH // A_HEADS
A_FDIM = A_HEADS * A_KEY
A_CHUNK = 64
B_HEADS = 8
B_HDIM = BRANCH_WIDTH // B_HEADS
B_CONV = 4
B_C = 8.0
C_HDIM = 64
C_HEADS = BRANCH_WIDTH // C_HDIM
C_GROUPS = 2
C_STATE = 128
C_CONV = 4
C_CHUNK = 128
C_CONV_DIM = BRANCH_WIDTH + 2 * C_GROUPS * C_STATE
SPLITS = (A_FDIM, A_FDIM, BRANCH_WIDTH, BRANCH_WIDTH, BRANCH_WIDTH, BRANCH_WIDTH, BRANCH_WIDTH, C_CONV_DIM, C_HEADS, N_BRANCH * D_MODEL)
IN_COLS_2 = sum(SPLITS)


def rmsnorm(x, w):
    xf = x.astype(jnp.float32)
    y = xf * lax.rsqrt(jnp.mean(xf * xf, axis=-1, keepdims=True) + EPS)
    return (y * w.astype(jnp.float32)).astype(x.dtype)

def causal_depthwise_conv(x, w, b):
    width, ch = w.shape
    y = lax.conv_general_dilated(x, w[:, None, :].astype(x.dtype), window_strides=(1,),
                                 padding=[(width - 1, 0)], dimension_numbers=('NWC', 'WIO', 'NWC'),
                                 feature_group_count=ch)
    return y + b.astype(x.dtype)

def hgrn2_mixer(q, f_pre, i, lb):
    bsz, s, _ = q.shape
    n = s // A_CHUNK
    lbf = lb.astype(jnp.float32)
    log_f = jnp.logaddexp(jnp.log(lbf), jnp.log1p(-lbf) + jax.nn.log_sigmoid(f_pre.astype(jnp.float32)))
    k = -jnp.expm1(log_f)

    def to_chunks(t, d):
        return t.astype(jnp.float32).reshape(bsz, n, A_CHUNK, A_HEADS, d).transpose(1, 0, 3, 2, 4)

    qc, kc, gc, vc = to_chunks(q, A_KEY), to_chunks(k, A_KEY), to_chunks(log_f, A_KEY), to_chunks(i, A_VAL)
    causal = jnp.tril(jnp.ones((A_CHUNK, A_CHUNK), dtype=bool))

    def step(state, inp):
        qb, kb, gb, vb = inp
        b = jnp.cumsum(gb, axis=-2)
        diff = b[:, :, :, None, :] - b[:, :, None, :, :]
        decay = jnp.exp(jnp.where(causal[:, :, None], diff, -jnp.inf))
        scores = jnp.einsum('bhtk,bhsk,bhtsk->bhts', qb, kb, decay)
        o = (jnp.einsum('bhts,bhsv->bhtv', scores, vb)
             + jnp.einsum('bhtk,bhkv->bhtv', qb * jnp.exp(b), state))
        b_last = b[:, :, -1:, :]
        state = (jnp.exp(b_last[:, :, 0, :, None]) * state
                 + jnp.einsum('bhsk,bhsv->bhkv', kb * jnp.exp(b_last - b), vb))
        return state, o

    s0 = jnp.zeros((bsz, A_HEADS, A_KEY, A_VAL), jnp.float32)
    _, o = lax.scan(step, s0, (qc, kc, gc, vc))
    return o.transpose(1, 0, 3, 2, 4).reshape(bsz, s, A_HEADS, A_VAL)

def rglru_mixer(x, conv_w, conv_b, wa, ba, wx, bx, lam):
    xc = causal_depthwise_conv(x, conv_w, conv_b)
    bsz, s, _ = xc.shape
    xh = xc.astype(jnp.float32).reshape(bsz, s, B_HEADS, B_HDIM)
    r = jax.nn.sigmoid(jnp.einsum('bshi,hij->bshj', xh, wa.astype(jnp.float32)) + ba).reshape(bsz, s, BRANCH_WIDTH)
    ig = jax.nn.sigmoid(jnp.einsum('bshi,hij->bshj', xh, wx.astype(jnp.float32)) + bx).reshape(bsz, s, BRANCH_WIDTH)
    log_a = -B_C * r * jax.nn.softplus(-lam.astype(jnp.float32))
    a = jnp.exp(log_a)
    u = jnp.sqrt(-jnp.expm1(2.0 * log_a)) * (ig * xh.reshape(bsz, s, BRANCH_WIDTH))

    def combine(left, right):
        a1, b1 = left
        a2, b2 = right
        return a1 * a2, a2 * b1 + b2

    _, h = lax.associative_scan(combine, (a, u), axis=1)
    return h

def segsum(x):
    t = x.shape[-1]
    cs = jnp.cumsum(x, axis=-1)
    mask = jnp.tril(jnp.ones((t, t), dtype=bool))
    return jnp.where(mask, cs[..., :, None] - cs[..., None, :], -jnp.inf)

def ssd_mixer(xbc_pre, dt_pre, conv_w, conv_b, dt_bias, a_log, d_skip):
    xbc = jax.nn.silu(causal_depthwise_conv(xbc_pre, conv_w, conv_b)).astype(jnp.float32)
    bsz, s, _ = xbc.shape
    n = s // C_CHUNK
    rep = C_HEADS // C_GROUPS
    xs, bm, cm = jnp.split(xbc, [BRANCH_WIDTH, BRANCH_WIDTH + C_GROUPS * C_STATE], axis=-1)
    xs = xs.reshape(bsz, n, C_CHUNK, C_GROUPS, rep, C_HDIM)
    bm = bm.reshape(bsz, n, C_CHUNK, C_GROUPS, C_STATE)
    cm = cm.reshape(bsz, n, C_CHUNK, C_GROUPS, C_STATE)
    dt = jax.nn.softplus(dt_pre.astype(jnp.float32) + dt_bias.astype(jnp.float32))
    a = -jnp.exp(a_log.astype(jnp.float32))
    dtc = dt.reshape(bsz, n, C_CHUNK, C_GROUPS, rep)
    da = (dtc * a.reshape(C_GROUPS, rep)).transpose(0, 3, 4, 1, 2)
    xdt = xs * dtc[..., None]
    cum = jnp.cumsum(da, axis=-1)
    lmat = jnp.exp(segsum(da))
    cb = jnp.einsum('bclgn,bcsgn->bgcls', cm, bm)
    y_diag = jnp.einsum('bgcls,bgrcls,bcsgrp->bclgrp', cb, lmat, xdt)
    decay_states = jnp.exp(cum[..., -1:] - cum)
    states = jnp.einsum('bclgn,bgrcl,bclgrp->bcgrpn', bm, decay_states, xdt)
    chunk_decay = jnp.exp(segsum(jnp.pad(cum[..., -1], [(0, 0), (0, 0), (0, 0), (1, 0)])))
    states = jnp.concatenate([jnp.zeros_like(states[:, :1]), states], axis=1)
    states = jnp.einsum('bgrzc,bcgrpn->bzgrpn', chunk_decay, states)[:, :-1]
    y_off = jnp.einsum('bclgn,bcgrpn,bgrcl->bclgrp', cm, states, jnp.exp(cum))
    y = y_diag + y_off + d_skip.astype(jnp.float32).reshape(C_GROUPS, rep)[:, :, None] * xs
    return y.reshape(bsz, s, BRANCH_WIDTH)

def second_inputs(seed: int = 0) -> dict:
    key = jax.random.key(seed)
    ks = jax.random.split(key, 24)
    f32 = jnp.float32

    def nrm(k, shape, scale):
        return scale * jax.random.normal(k, shape, f32)

    x = jax.random.normal(ks[0], (BATCH, SEQ, D_MODEL), f32)
    norm_w = 1.0 + nrm(ks[1], (DEPTH, D_MODEL), 0.02)
    w_in = nrm(ks[2], (DEPTH, D_MODEL, IN_COLS_2), D_MODEL ** -0.5)
    hgrn_lb_logits = nrm(ks[3], (DEPTH, A_FDIM), 0.5)
    hgrn_norm_w = 1.0 + nrm(ks[4], (DEPTH, BRANCH_WIDTH), 0.02)
    rglru_conv_w = nrm(ks[5], (DEPTH, B_CONV, BRANCH_WIDTH), B_CONV ** -0.5)
    rglru_conv_b = nrm(ks[6], (DEPTH, BRANCH_WIDTH), 0.02)
    rglru_wa = nrm(ks[7], (DEPTH, B_HEADS, B_HDIM, B_HDIM), B_HDIM ** -0.5)
    rglru_ba = nrm(ks[8], (DEPTH, B_HEADS, B_HDIM), 0.02)
    rglru_wx = nrm(ks[9], (DEPTH, B_HEADS, B_HDIM, B_HDIM), B_HDIM ** -0.5)
    rglru_bx = nrm(ks[10], (DEPTH, B_HEADS, B_HDIM), 0.02)
    u = jax.random.uniform(ks[11], (DEPTH, BRANCH_WIDTH), f32, 0.9, 0.999)
    p = u ** (1.0 / B_C)
    rglru_lambda = jnp.log(p) - jnp.log1p(-p)
    ssd_conv_w = nrm(ks[12], (DEPTH, C_CONV, C_CONV_DIM), C_CONV ** -0.5)
    ssd_conv_b = nrm(ks[13], (DEPTH, C_CONV_DIM), 0.02)
    dt0 = jnp.exp(jax.random.uniform(ks[14], (DEPTH, C_HEADS), f32, float(np.log(1e-3)), float(np.log(1e-1))))
    ssd_dt_bias = dt0 + jnp.log(-jnp.expm1(-dt0))
    ssd_a_log = jnp.log(jax.random.uniform(ks[15], (DEPTH, C_HEADS), f32, 1.0, 16.0))
    ssd_d = 1.0 + nrm(ks[16], (DEPTH, C_HEADS), 0.1)
    ssd_norm_w = 1.0 + nrm(ks[17], (DEPTH, BRANCH_WIDTH), 0.02)
    w_out = nrm(ks[18], (DEPTH, N_BRANCH * BRANCH_WIDTH, D_MODEL), (N_BRANCH * BRANCH_WIDTH) ** -0.5)
    final_norm_w = 1.0 + nrm(ks[19], (D_MODEL,), 0.02)
    return {'x': x, 'norm_w': norm_w, 'w_in': w_in, 'hgrn_lb_logits': hgrn_lb_logits,
            'hgrn_norm_w': hgrn_norm_w, 'rglru_conv_w': rglru_conv_w, 'rglru_conv_b': rglru_conv_b,
            'rglru_wa': rglru_wa, 'rglru_ba': rglru_ba, 'rglru_wx': rglru_wx, 'rglru_bx': rglru_bx,
            'rglru_lambda': rglru_lambda, 'ssd_conv_w': ssd_conv_w, 'ssd_conv_b': ssd_conv_b,
            'ssd_dt_bias': ssd_dt_bias, 'ssd_a_log': ssd_a_log, 'ssd_d': ssd_d, 'ssd_norm_w': ssd_norm_w,
            'w_out': w_out, 'final_norm_w': final_norm_w}

def second_block(x, norm_w, w_in, hgrn_lb_logits, hgrn_norm_w, rglru_conv_w, rglru_conv_b, rglru_wa, rglru_ba,
              rglru_wx, rglru_bx, rglru_lambda, ssd_conv_w, ssd_conv_b, ssd_dt_bias, ssd_a_log, ssd_d,
              ssd_norm_w, w_out, final_norm_w):
    split_idx = np.cumsum(SPLITS)[:-1].tolist()
    sm = jax.nn.softmax(hgrn_lb_logits.astype(jnp.float32), axis=0)
    cs = jnp.cumsum(sm, axis=0)
    lower_bounds = cs - cs[0:1]
    bsz, s, _ = x.shape
    for l in range(DEPTH):
        h = rmsnorm(x, norm_w[l])
        proj = h @ w_in[l]
        a_q, a_f, a_i, a_z, b_x, b_z, c_z, c_xbc, c_dt, gate_logits = jnp.split(proj, split_idx, axis=-1)
        o_a = hgrn2_mixer(a_q, a_f, a_i, lower_bounds[l])
        o_a = rmsnorm(o_a, hgrn_norm_w[l].reshape(A_HEADS, A_VAL)).reshape(bsz, s, BRANCH_WIDTH)
        o_a = o_a * jax.nn.silu(a_z)
        o_b = rglru_mixer(b_x, rglru_conv_w[l], rglru_conv_b[l], rglru_wa[l], rglru_ba[l], rglru_wx[l],
                          rglru_bx[l], rglru_lambda[l]) * jax.nn.silu(b_z)
        y_c = ssd_mixer(c_xbc, c_dt, ssd_conv_w[l], ssd_conv_b[l], ssd_dt_bias[l], ssd_a_log[l], ssd_d[l])
        o_c = rmsnorm((y_c * jax.nn.silu(c_z)).reshape(bsz, s, C_GROUPS, BRANCH_WIDTH // C_GROUPS),
                      ssd_norm_w[l].reshape(C_GROUPS, BRANCH_WIDTH // C_GROUPS)).reshape(bsz, s, BRANCH_WIDTH)
        branches = jnp.stack([o_a, o_b, o_c], axis=2).astype(x.dtype)
        branch_out = jnp.einsum('bsnc,ncd->bsnd', branches,
                                w_out[l].reshape(N_BRANCH, BRANCH_WIDTH, D_MODEL))
        gates = jax.nn.sigmoid(gate_logits.astype(jnp.float32).reshape(bsz, s, N_BRANCH, D_MODEL))
        x = x + jnp.sum(gates * branch_out, axis=2).astype(x.dtype)
    return rmsnorm(x, final_norm_w)


_first_inputs = second_inputs


def second_inputs(seed=0):
    import zlib

    import numpy as np

    out = dict(_first_inputs(seed))
    spreads = {}
    factors = {'norm_w': 4.31,
     'hgrn_norm_w': 8.0,
     'rglru_conv_b': 4.076,
     'rglru_ba': 8.0,
     'rglru_bx': 8.0,
     'ssd_conv_b': 7.529,
     'ssd_norm_w': 8.0,
     'final_norm_w': 2.913}
    for name, (base, spread) in spreads.items():
        noise = np.random.default_rng([zlib.crc32(name.encode()), seed]).standard_normal(out[name].shape)
        drawn = base * np.exp(spread * noise) if base else spread * noise
        out[name] = jnp.asarray(drawn.astype(out[name].dtype))
    for name, factor in factors.items():
        out[name] = (out[name] * factor).astype(out[name].dtype)
    return out


_narrow_inputs = second_inputs


def second_inputs(seed=0):

    out = dict(_narrow_inputs(seed))
    wider = {'hgrn_norm_w': 3.66,
     'rglru_ba': 9.81,
     'rglru_bx': 7.06,
     'ssd_conv_b': 5.18,
     'ssd_d': 12.0,
     'ssd_norm_w': 10.93,
     'final_norm_w': 3.26}
    for name, times in wider.items():
        mean = out[name].mean()
        out[name] = (mean + times * (out[name] - mean)).astype(out[name].dtype)
    return out


def setup_inputs(seed=0):
    out = dict(first_inputs(seed))
    for name, value in second_inputs(seed + 1).items():
        if name != "x":
            out[name + "_2"] = value
    return out


def reference(
    x, c, ctx, c_ctx, w_mod, b_mod, norm1_g, norm2_g, w_in, conv_w, conv_b, conv_ln_g,
    conv_ln_b, w_conv_out, dn_short_w, dn_a_log, dn_dt_bias, dn_norm_g, w_dn_out, w_out,
    peer_w_q, peer_key1, peer_key2, peer_u, peer_v, final_g, norm_w_2, w_in_2, hgrn_lb_logits_2,
    hgrn_norm_w_2, rglru_conv_w_2, rglru_conv_b_2, rglru_wa_2, rglru_ba_2, rglru_wx_2,
    rglru_bx_2, rglru_lambda_2, ssd_conv_w_2, ssd_conv_b_2, ssd_dt_bias_2, ssd_a_log_2, ssd_d_2,
    ssd_norm_w_2, w_out_2, final_norm_w_2,
):
    x = first_block(
        x, c, ctx, c_ctx, w_mod, b_mod, norm1_g, norm2_g, w_in, conv_w, conv_b, conv_ln_g,
        conv_ln_b, w_conv_out, dn_short_w, dn_a_log, dn_dt_bias, dn_norm_g, w_dn_out, w_out,
        peer_w_q, peer_key1, peer_key2, peer_u, peer_v, final_g,
    )
    return second_block(
        x, norm_w_2, w_in_2, hgrn_lb_logits_2, hgrn_norm_w_2, rglru_conv_w_2, rglru_conv_b_2,
        rglru_wa_2, rglru_ba_2, rglru_wx_2, rglru_bx_2, rglru_lambda_2, ssd_conv_w_2,
        ssd_conv_b_2, ssd_dt_bias_2, ssd_a_log_2, ssd_d_2, ssd_norm_w_2, w_out_2,
        final_norm_w_2,
    )


_drawn_inputs = setup_inputs


def setup_inputs(seed=0):
    import zlib

    import numpy as np

    out = dict(_drawn_inputs(seed))
    spreads = {}
    factors = {'conv_b': 3.73,
     'conv_ln_g': 2.973,
     'conv_ln_b': 5.666,
     'dn_norm_g': 3.004,
     'ssd_d_2': 28.961}
    for name, (base, spread) in spreads.items():
        noise = np.random.default_rng([zlib.crc32(name.encode()), seed]).standard_normal(out[name].shape)
        drawn = base * np.exp(spread * noise) if base else spread * noise
        out[name] = jnp.asarray(drawn.astype(out[name].dtype))
    for name, factor in factors.items():
        out[name] = (out[name] * factor).astype(out[name].dtype)
    return out
```

```python
import concourse.bass as bass
from concourse import mybir
from contextlib import ExitStack

P = 128
D = 2048
KT = D // P
L = 256
EPS = 1e-6
SLOTS = 4
HEADS = 16
SHORT = 5
WIDTH = 31
ROWW = 64
NEG = -3.0e38

F32 = mybir.dt.float32
F32R = mybir.dt.float32r
U32 = mybir.dt.uint32
ACT = mybir.ActivationFunctionType
ALU = mybir.AluOpType
AX = mybir.AxisListType

COLS = [("c", 16), ("c_ctx", 16), ("norm1_g", 16), ("norm2_g", 16), ("b_mod", 96), ("conv_b", 16),
        ("ln_g", 16), ("ln_b", 16), ("dn_g", 1), ("final_g", 16), ("norm_w", 16), ("hgrn_g", 8),
        ("rg_cb", 8), ("rg_cw", 32), ("ba", 8), ("bx", 8), ("lam", 8), ("ssd_cw", 48), ("ssd_cb", 12),
        ("ssd_g", 8), ("final_w", 16), ("ssd_d", 8), ("dn_alog", 1), ("dn_dtb", 1), ("ssd_alog", 1),
        ("ssd_dtb", 1)]
COL_AT = {}
_n = 0
for _name, _w in COLS:
    COL_AT[_name] = (_n, _n + _w)
    _n += _w
NCOLS = _n


def flat(ap):
    return ap.rearrange("p s c -> p (s c)")


class Core:

    def __init__(self, nc, ctx, inputs):
        self.nc, self.i = nc, inputs
        sb = lambda name, shape: ctx.enter_context(nc.sbuf_tensor(name, shape, F32))
        sem = lambda name: ctx.enter_context(nc.semaphore(name))
        at = -(-nc.sbuf_base // 32) * 32
        self.arena = sb("arena", [P, 200, L])
        self.rounded = [nc.alloc_sbuf_tensor_at(f"rounded{q}", [P, 4, L], F32R, offset=at + q * 4 * L * 4)
                        for q in range(50)]
        self.dt_raw = sb("dt_raw", [P, L])
        self.cols = sb("cols", [P, NCOLS])
        self.cst = sb("cst", [P, 2 * P])
        self.ident, self.ones = self.cst[:, 0:P], self.cst[:, P:2 * P]
        self.silu_c = sb("silu_c", [P, 32])
        self.mod_x, self.mod_c = sb("mod_x", [P, 96]), sb("mod_c", [P, 32])
        self.gain1, self.gain2 = sb("gain1", [P, 32]), sb("gain2", [P, 16])
        self.eps, self.neg_a = sb("eps", [P, 2]), sb("neg_a", [P, 1])
        self.gst = sb("gst", [P, 4, 2])[:]
        self.ps = [ctx.enter_context(nc.psum_tensor(f"bank{b}", [P, 512], F32)) for b in range(8)]
        self.iota = self.t(195, 1)[:, 0, 0:P]
        self.rstd = self.t(195, 2).rearrange("p s c -> p (s c)")
        self.gb = self.t(197, 1)[:, 0, :].rearrange("p (c r) -> p c r", c=4)
        tables = self.t(198, 2).rearrange("p s (m c) -> p (s m) c", m=2)
        self.gsum, self.kdec, self.etot, self.negegc = (tables[:, m, :] for m in range(4))
        self.slot_loaded = [sem(f"weights_in_slot{r}") for r in range(SLOTS)]
        self.tile_done, self.tile_out = sem("tile_done"), sem("tile_out")
        self.tokens_in, self.taps_in, self.eps_set = sem("tokens_in"), sem("taps_in"), sem("eps_set")
        self.raw_loaded = [sem(f"weights_in_raw{r}") for r in range(2)]
        self.hi_done, self.lo_done, self.half_done = sem("weights_hi"), sem("weights_lo"), sem("half_multiplied")
        self.seq = self.evacs = self.raws = 0
        self.stage_sems = {}

    def sem(self, stage, name):
        if stage not in self.stage_sems:
            taken = self.stage_sems[stage] = []

            def finish():
                self.nc.clear_and_free_semaphores(taken)
                self.nc.all_engine_barrier()

            stage.callback(finish)
        self.stage_sems[stage].append(self.nc.alloc_semaphore(name))
        return self.stage_sems[stage][-1]

    def t(self, slot, n):
        return self.arena[:, slot:slot + n, :]

    def r(self, slot, n):
        return self.rounded[slot // 4][:, slot % 4:slot % 4 + n, :]

    def raw(self, r):
        return self.ring(r)

    def staged(self, part, b):
        return self.r(16 + 8 * b + 4 * part, 4).rearrange("p s c -> p (s c)")

    def ring(self, r):
        return self.t(8 * r, 8).rearrange("p s c -> p (s c)")

    def out(self, b, n):
        return self.ps[b][:, 0:n] if n <= L else self.ps[b][:, 0:n].rearrange("p (a c) -> p a c", a=2)

    def col(self, name):
        a, b = COL_AT[name]
        return self.cols[:, a:b]

    def x_ctx(self, part):
        return self.t(64, 32).rearrange("p (t s) c -> p t (s c)", s=2)[:, :, part]

    def hx(self, kt):
        return self.t(32, 32).rearrange("p (s t) c -> p s t c", s=2)[:, :, kt, :]

    def key_tile(self, h):
        return self.t(80, 32)[:, bass.ds(h * 2, 2), :].rearrange("p s c -> p (s c)")

    def value_tile(self, h):
        return self.t(112, 32)[:, bass.ds(h * 2, 2), :].rearrange("p s c -> p (s c)")

    def query_tile(self, h):
        return self.t(160, 16)[:, bass.ds(h, 1), :].rearrange("p s c -> p (s c)")


def side_nothing(k):
    return {}


def linear(k, name, w, tiles, rhs, n, evac_on, evac, following=None, side=None, following3=None):
    nc = k.nc
    side = side or {}
    s0, e0 = k.seq, k.evacs
    groups = tiles // SLOTS

    with ExitStack() as stage:
        if "sems" in side:
            side["sems"](stage)
        block = stage.enter_context(nc.Block())

        @block.sync
        def _(sp):
            def load(src, slot, need):
                sp.wait_ge(k.tile_done, need)
                sp.dma_start(k.ring(slot), src).then_inc(k.slot_loaded[slot], 16)

            if groups > 1:
                with sp.Fori(1, groups) as g:
                    for r in range(SLOTS):
                        load(w[bass.ds(g * SLOTS + r, 1)].rearrange("a p n -> (a p) n"), r,
                             g * SLOTS + (s0 + r + 1 - SLOTS))
            if following is not None:
                for r in range(min(SLOTS, following.shape[0])):
                    load(following[r], r, s0 + tiles - SLOTS + r + 1)
            if following3 is not None:
                for r in range(2):
                    sp.wait_ge(k.tile_done, s0 + tiles - SLOTS + r + 1)
                    sp.dma_start(k.raw(r), following3[r]).then_inc(k.raw_loaded[r], 16)
            if "sync" in side:
                side["sync"](sp)

        @block.tensor
        def _(pe):
            def group(g, first):
                for r in range(SLOTS):
                    pe.wait_ge(k.slot_loaded[r], g * 16 + (16 * (s0 // SLOTS) + 16))
                    if not first:
                        pe.wait_ge(k.tile_out, g * SLOTS + (e0 + r + 1 - SLOTS))
                    for kt in range(KT):
                        mm = pe.matmul(k.out(r, n), k.ring(r)[:, kt * P:(kt + 1) * P], rhs(kt),
                                       start=(kt == 0), stop=(kt == KT - 1))
                    mm.then_inc(k.tile_done, 1)

            group(0, True)
            if groups > 1:
                with pe.Fori(1, groups) as g:
                    group(g, False)

        def evacuate(eng):
            with eng.Fori(0, groups) as g:
                for r in range(SLOTS):
                    eng.wait_ge(k.tile_done, g * SLOTS + (s0 + r + 1))
                    evac(eng, g * SLOTS + r, k.ps[r][:, 0:n]).then_inc(k.tile_out, 1)

        if evac_on == "scalar":
            @block.scalar
            def _(act):
                evacuate(act)
                if "scalar" in side:
                    side["scalar"](act)

            if "vector" in side:
                @block.vector
                def _(dve):
                    side["vector"](dve)
        else:
            @block.vector
            def _(dve):
                evacuate(dve)

            if "scalar" in side:
                @block.scalar
                def _(act):
                    side["scalar"](act)

        if "gpsimd" in side:
            @block.gpsimd
            def _(pool):
                side["gpsimd"](pool)

    k.seq += tiles
    k.evacs += tiles


def split(k, name, src, hi, lo, slots=KT):
    with ExitStack() as stage:
        high, low = k.sem(stage, f"{name}_high"), k.sem(stage, f"{name}_low")
        block = stage.enter_context(k.nc.Block())

        @block.scalar
        def _(act):
            for q in range(0, slots, 4):
                act.activation(k.r(hi + q, 4), k.t(src + q, 4), ACT.Copy).then_inc(high, 1)

        @block.vector
        def _(dve):
            for q in range(0, slots, 4):
                dve.wait_ge(high, q // 4 + 1)
                dve.tensor_tensor(k.r(lo + q, 4), k.t(src + q, 4), k.r(hi + q, 4), ALU.subtract).then_inc(low, 1)


def make_high(k, act, g, r, q, s, first):
    b, c = q, slice(q * 1024, (q + 1) * 1024)
    if q == 0:
        act.wait_ge(k.raw_loaded[r % 2], g * 32 + (16 * ((s + r) // 2) + 16))
    if not (first and r == 0):
        act.wait_ge(k.half_done, g * (2 * SLOTS) + (2 * (s + r) + q - 1))
    act.activation(k.staged(0, b), k.raw(r % 2)[:, c], ACT.Copy).then_inc(k.hi_done, 1)


def make_low(k, dve, g, r, q, s):
    c = slice(q * 1024, (q + 1) * 1024)
    dve.wait_ge(k.hi_done, g * (2 * SLOTS) + (2 * (s + r) + q + 1))
    dve.tensor_tensor(k.staged(1, q), k.raw(r % 2)[:, c], k.staged(0, q), ALU.subtract).then_inc(k.lo_done, 1)


def load_raw(k, sp, w, tiles, s):
    def load(src, r, need):
        sp.wait_ge(k.lo_done, need)
        sp.dma_start(k.raw(r % 2), src).then_inc(k.raw_loaded[r % 2], 16)

    for r in range(2, SLOTS):
        load(w[r], r, 2 * (s + r - 2) + 2)
    if tiles > SLOTS:
        with sp.Fori(1, tiles // SLOTS) as g:
            for r in range(SLOTS):
                load(w[bass.ds(g * SLOTS + r, 1)].rearrange("a p n -> (a p) n"), r,
                     g * (2 * SLOTS) + (2 * (s + r - 2) + 2))


def load_next(k, sp, following, following3, s_end):
    for r in range(2 if following is None else SLOTS):
        src = following3 if following is None else following
        if src is None:
            break
        sp.wait_ge(k.lo_done, 2 * (s_end - 2 + r % 2) + 2)
        if r >= 2:
            sp.wait_ge(k.half_done, 2 * s_end)
        sem = k.raw_loaded[r] if following is None else k.slot_loaded[r]
        sp.dma_start(k.ring(r), src[r]).then_inc(sem, 16)


def linear3(k, name, w, tiles, hi, lo, evac_on, evac, following3=None, side=None, pairs=False, following=None):
    nc = k.nc
    side = side or {}
    s, e0 = k.raws, k.evacs
    groups = tiles // SLOTS
    n = L
    with ExitStack() as stage:
        block = stage.enter_context(nc.Block())

        @block.sync
        def _(sp):
            if "sync" in side:
                side["sync"](sp)
            load_raw(k, sp, w, tiles, s)
            load_next(k, sp, following, following3, s + tiles)

        @block.tensor
        def _(pe):
            def group(g, first):
                for r in range(SLOTS):
                    if not first:
                        pe.wait_ge(k.tile_out, g * SLOTS + (e0 + r + 1 - SLOTS))
                    for q in range(2):
                        pe.wait_ge(k.lo_done, g * (2 * SLOTS) + (2 * (s + r) + q + 1))
                        for j in range(8):
                            wh, wl = (k.staged(m, q)[:, j * P:(j + 1) * P] for m in range(2))
                            kt = j if pairs else 8 * q + j
                            out = k.ps[r][:, q * n:(q + 1) * n] if pairs else k.ps[r][:, 0:n]
                            fresh = j == 0 and (pairs or q == 0)
                            end = j == 7 and (pairs or q == 1)
                            pe.matmul(out, wh, hi(kt), start=fresh, stop=False)
                            pe.matmul(out, wh, lo(kt), start=False, stop=False)
                            mm = pe.matmul(out, wl, hi(kt), start=False, stop=end)
                        mm.then_inc(k.half_done, 1)

            group(0, True)
            if groups > 1:
                with pe.Fori(1, groups) as g:
                    group(g, False)

        def write_out(eng, j, r, done):
            eng.wait_ge(k.half_done, done)
            evac(eng, j, k.ps[r][:, 0:2 * n if pairs else n]).then_inc(k.tile_out, 1)

        def engine(eng, make, evacuates):
            def group(g, first):
                for r in range(SLOTS):
                    make(g, r, first)
                    if evacuates and not (first and r == 0):
                        write_out(eng, g * SLOTS + (r - 1), (r - 1) % SLOTS, g * (2 * SLOTS) + 2 * (s + r))

            group(0, True)
            if groups > 1:
                with eng.Fori(1, groups) as g:
                    group(g, False)
            if evacuates:
                write_out(eng, tiles - 1, SLOTS - 1, 2 * (s + tiles))

        @block.scalar
        def _(act):
            def make(g, r, first):
                for q in range(2):
                    make_high(k, act, g, r, q, s, first)

            engine(act, make, evac_on == "scalar")

        @block.vector
        def _(dve):
            def make(g, r, first):
                for q in range(2):
                    make_low(k, dve, g, r, q, s)

            engine(dve, make, evac_on == "vector")

    k.raws += tiles
    k.evacs += tiles


def prologue(k, first_weights):
    nc = k.nc
    CH = 512
    NCH = 6 * D // CH
    NCTX = 2 * D // CH
    HALF = 4

    with ExitStack() as stage:
        sem = lambda n: k.sem(stage, n)
        cols_in, chunk_in = sem("cols_in"), [sem(f"mod_chunk_in{i}") for i in range(8)]
        silu_done, step, summed, out_done = sem("silu_done"), sem("mod_step"), sem("mod_summed"), sem("mod_out")
        acc = k.t(160, 32).rearrange("p s c -> p (s c)")[:, 0:8 * CH].rearrange(
            "p (a b e c) -> p a b e c", a=2, b=2, e=2)
        block = stage.enter_context(nc.Block())

        def slot8(i):
            return k.t(8 * i, 8).rearrange("p s c -> p (s c)")

        def steps_before(n):
            return 32 * n if n <= NCTX else 32 * NCTX + 16 * (n - NCTX)

        @block.sync
        def _(sp):
            sp.dma_start(k.cols[:], k.i["cols"]).then_inc(cols_in, 16)
            sp.dma_start(k.cst[:], k.i["cst"][:, 0:256]).then_inc(cols_in, 16)
            for q in range(8):
                sp.dma_start(slot8(q), k.i["w_mod"][q]).then_inc(chunk_in[q], 16)
            sp.dma_start(k.x_ctx(slice(0, L)), k.i["x"]).then_inc(k.tokens_in, 16)
            sp.dma_start(k.x_ctx(slice(L, 2 * L)), k.i["ctx"]).then_inc(k.tokens_in, 16)

            def chunks(pair, nb, base):
                for a in range(2):
                    for q in range(HALF):
                        i = a * HALF + q
                        sp.wait_ge(step, pair * (2 * 16 * nb) + (base + 16 * nb * a + 4 * nb * (q + 1)))
                        sp.dma_start(slot8(i), k.i["w_mod"][bass.ds(pair * 8 + (i + 8), 1)].rearrange(
                            "a p n -> (a p) n")).then_inc(chunk_in[i], 16)

            with sp.Fori(0, NCTX // 2) as pair:
                chunks(pair, 2, 0)
            with sp.Fori(NCTX // 2, NCH // 2 - 1) as pair:
                chunks(pair, 1, steps_before(NCTX) - 16 * NCTX)
            sp.wait_ge(step, steps_before(NCH))
            for r in range(2):
                sp.dma_start(k.raw(r), first_weights[r]).then_inc(k.raw_loaded[r], 16)

        @block.gpsimd
        def _(pool):
            pool.memset(k.eps[:, 0:1], EPS).then_inc(k.eps_set, 1)
            pool.memset(k.eps[:, 1:2], P * EPS).then_inc(k.eps_set, 1)

        @block.scalar
        def _(act):
            act.wait_ge(k.eps_set, 2)
            act.wait_ge(cols_in, 32)
            act.activation(k.silu_c[:], k.cols[:, 0:32], ACT.Silu).then_inc(silu_done, 1)

        @block.vector
        def _(dve):
            dve.wait_ge(silu_done, 1)

            def pair_of_chunks(pair, nb, base, first):
                for a in range(2):
                    for q in range(HALF):
                        i = a * HALF + q
                        dve.wait_ge(chunk_in[i], pair * 16 + 16)
                        if q == 0 and not first:
                            dve.wait_ge(summed, pair * 2 + (a - 1))
                        for j in range(4):
                            kt = 4 * q + j
                            for b in range(nb):
                                at = 16 * nb * a + nb * kt + b
                                out = acc[:, a, b, kt % 2, :]
                                rows = slot8(i)[:, j * CH:(j + 1) * CH]
                                s = k.silu_c[:, 16 * b + kt:16 * b + kt + 1]
                                if kt < 2:
                                    ins = dve.tensor_scalar(out, rows, s, None, ALU.mult)
                                else:
                                    dve.wait_ge(step, pair * (32 * nb) + (base + at - 2 * nb + 1))
                                    ins = dve.scalar_tensor_tensor(out=out, in0=rows, scalar=s, in1=out,
                                                                   op0=ALU.mult, op1=ALU.add)
                                ins.then_inc(step, 1)

            pair_of_chunks(0, 2, 0, True)
            with dve.Fori(1, NCTX // 2) as pair:
                pair_of_chunks(pair, 2, 0, False)
            with dve.Fori(NCTX // 2, NCH // 2) as pair:
                pair_of_chunks(pair, 1, steps_before(NCTX) - 16 * NCTX, False)
            b0 = COL_AT["b_mod"][0]
            dve.wait_ge(summed, NCH)
            dve.tensor_tensor(k.mod_x[:], k.ps[0][:, 0:96], k.cols[:, b0:b0 + 96], ALU.add).then_inc(out_done, 1)
            dve.tensor_tensor(k.mod_c[:], k.ps[1][:, 0:32], k.cols[:, b0:b0 + 32], ALU.add).then_inc(out_done, 1)
            dve.wait_ge(out_done, 2)
            one = k.mod_x[:, 16:32]
            for gain, scale, g in ((k.gain1[:, 0:16], k.mod_x[:, 16:32], "norm1_g"),
                                   (k.gain1[:, 16:32], k.mod_c[:, 16:32], "norm1_g"),
                                   (k.gain2[:], k.mod_x[:, 64:80], "norm2_g")):
                dve.scalar_tensor_tensor(out=gain, in0=scale, scalar=1.0, in1=k.col(g), op0=ALU.add,
                                         op1=ALU.mult).then_inc(out_done, 1)

        @block.tensor
        def _(pe):
            pe.wait_ge(cols_in, 32)

            def sums(pair, nb, base):
                for a in range(2):
                    pe.wait_ge(step, pair * (32 * nb) + (base + 16 * nb * (a + 1)))
                    for b in range(nb):
                        for m in range(4):
                            for e in range(2):
                                mm = pe.matmul(k.ps[b][:, bass.ds(pair * 8 + (4 * a + m), 1)],
                                               acc[:, a, b, e, m * P:(m + 1) * P], k.ones[:, 0:1],
                                               start=(e == 0), stop=(e == 1))
                    mm.then_inc(summed, 1)

            with pe.Fori(0, NCTX // 2) as pair:
                sums(pair, 2, 0)
            with pe.Fori(NCTX // 2, NCH // 2) as pair:
                sums(pair, 1, steps_before(NCTX) - 16 * NCTX)


def rms_norm(k, name, src, dst, tmp, n, parts, wait_tokens=False):
    nc = k.nc
    with ExitStack() as stage:
        sem = lambda s: k.sem(stage, f"{name}_{s}")
        squared, added, root, inverse, scaled, written = (sem(s) for s in (
            "squared", "added", "root", "inverse", "scaled", "written"))
        block = stage.enter_context(nc.Block())

        @block.vector
        def _(dve):
            if wait_tokens:
                dve.wait_ge(k.tokens_in, 32)
            for t in range(KT):
                if t >= 2:
                    dve.wait_ge(added, t - 1)
                dve.tensor_tensor(tmp(t % 2), src(t), src(t), ALU.mult).then_inc(squared, 1)
            dve.wait_ge(root, 1)
            dve.reciprocal(k.rstd[:, 0:n], k.rstd[:, 0:n]).then_inc(inverse, 1)
            dve.wait_ge(inverse, 1)
            for t in range(KT):
                if t >= 2:
                    dve.wait_ge(scaled, t - 1)
                    dve.wait_ge(written, len(parts) * (t - 1))
                dve.tensor_tensor(tmp(t % 2), src(t), k.rstd[:, 0:n], ALU.mult).then_inc(scaled, 1)

        @block.tensor
        def _(pe):
            for t in range(KT):
                pe.wait_ge(squared, t + 1)
                pe.matmul(k.ps[0][:, 0:n], k.ones[:], tmp(t % 2), start=(t == 0),
                          stop=(t == KT - 1)).then_inc(added, 1)

        @block.scalar
        def _(act):
            act.wait_ge(added, KT)
            act.activation(k.rstd[:, 0:n], k.ps[0][:, 0:n], ACT.Sqrt, bias=k.eps[:, 0:1],
                           scale=1.0 / D).then_inc(root, 1)
            for t in range(KT):
                act.wait_ge(scaled, t + 1)
                for a, b, gain, shift in parts:
                    bias = shift[:, t:t + 1] if shift is not None else 0.0
                    act.activation(dst(t, a), tmp(t % 2)[:, a:b], ACT.Identity, bias=bias,
                                   scale=gain[:, t:t + 1]).then_inc(written, 1)


def grid_conv_side(k):
    out = {}

    def sems(stage):
        out["conv_step"] = k.sem(stage, "grid_conv_step")

    def vector(dve):
        step = out["conv_step"]
        src = k.t(64, 16).rearrange("p s (r w) -> p s r w", w=ROWW)
        dst = k.t(144, 16).rearrange("p s (r w) -> p s r w", w=ROWW)
        half = WIDTH // 2
        taps = [half] + [q for q in range(WIDTH) if q != half]
        b0 = COL_AT["conv_b"][0]
        dve.wait_ge(k.taps_in, 32)
        with dve.Fori(0, KT // 2) as pair:
            for n, q in enumerate(taps):
                for a in range(2):
                    at = bass.ds(pair * 2 + a, 1)
                    w = k.t(192, 2).rearrange("p s c -> p (s c)")[:, bass.ds((pair * 2 + a) * WIDTH + q, 1)]
                    if n == 0:
                        ins = dve.tensor_scalar(k.t(144, 16)[:, at, :].rearrange("p s c -> p (s c)"),
                                                k.t(64, 16)[:, at, :].rearrange("p s c -> p (s c)"),
                                                w, k.cols[:, bass.ds(pair * 2 + (b0 + a), 1)],
                                                ALU.mult, ALU.add)
                    else:
                        dve.wait_ge(step, pair * (2 * WIDTH) + (2 * n + a - 1))
                        s = q - half
                        lo, hi = max(0, -s), ROWW - max(0, s)
                        o = dst[:, at, :, lo:hi].rearrange("p s r w -> p (s r) w")
                        i = src[:, at, :, lo + s:hi + s].rearrange("p s r w -> p (s r) w")
                        ins = dve.scalar_tensor_tensor(out=o, in0=i, scalar=w, in1=o, op0=ALU.mult,
                                                       op1=ALU.add)
                    ins.then_inc(step, 1)

    return {"sems": sems, "vector": vector}


def short_conv_side(k):
    out = {}

    def sems(stage):
        for n in ("added", "copied"):
            out[n] = k.sem(stage, f"short_conv_{n}")

    half = SHORT // 2
    PARTS = ((80, 2, 32, 16), (160, 1, 16, 0))

    def tmp(b, n):
        return k.t(176 + 2 * b, 2).rearrange("p s c -> p (s c)")[:, 0:n]

    def tile(slot, width, j):
        return k.t(slot, 32 * 2 if width == 2 else 16)[:, bass.ds(j * width, width), :]

    def vector(dve):
        base = 0
        for slot, width, tiles, w0 in PARTS:
            with dve.Fori(0, tiles // 4) as g:
                for n, q in enumerate([half] + [q for q in range(SHORT) if q != half]):
                    for b in range(4):
                        j = g * 4 + b
                        w = k.t(194, 1)[:, 0, bass.ds((j + w0) * SHORT + q, 1)]
                        t = tile(slot, width, j)
                        o = tmp(b, width * L).rearrange("p (s c) -> p s c", s=width)
                        if n == 0:
                            dve.wait_ge(out["copied"], g * 4 + (base // SHORT + b + 1))
                            ins = dve.tensor_scalar(o, t, w, None, ALU.mult)
                        else:
                            s = q - half
                            lo, hi = max(0, -s), L - max(0, s)
                            dve.wait_ge(out["added"], g * (4 * SHORT) + (base + 4 * (n - 1) + b + 1))
                            ins = dve.scalar_tensor_tensor(out=o[:, :, lo:hi], in0=t[:, :, lo + s:hi + s],
                                                           scalar=w, in1=o[:, :, lo:hi], op0=ALU.mult,
                                                           op1=ALU.add)
                        ins.then_inc(out["added"], 1)
            base += tiles * SHORT

    def gpsimd(pool):
        pool.sem_inc(out["copied"], 4)
        base = 0
        for slot, width, tiles, w0 in PARTS:
            with pool.Fori(0, tiles // 4) as g:
                for b in range(4):
                    j = g * 4 + b
                    pool.wait_ge(out["added"], g * (4 * SHORT) + (base + 4 * (SHORT - 1) + b + 1))
                    pool.tensor_copy(tile(slot, width, j),
                                     tmp(b, width * L).rearrange("p (s c) -> p s c", s=width)
                                     ).then_inc(out["copied"], 1)
            base += tiles * SHORT

    return {"sems": sems, "vector": vector, "gpsimd": gpsimd}


def layer_norm_silu(k, slot):
    nc = k.nc
    x = lambda t: k.t(slot, 16)[:, t, :]
    tmp = lambda b: k.t(176 + b, 1)[:, 0, :]
    mean = k.t(178, 1)[:, 0, :]
    with ExitStack() as stage:
        sem = lambda s: k.sem(stage, f"ln_{s}")
        summed, meaned, centred, squared, added, root, inverse, scaled, written = (sem(s) for s in (
            "summed", "mean", "centred", "squared", "added", "root", "inverse", "scaled", "written"))
        block = stage.enter_context(nc.Block())

        @block.tensor
        def _(pe):
            for t in range(KT):
                mm = pe.matmul(k.ps[1][:, 0:L], k.ones[:], x(t), start=(t == 0), stop=(t == KT - 1))
            mm.then_inc(summed, 1)
            for t in range(KT):
                pe.wait_ge(squared, t + 1)
                pe.matmul(k.ps[0][:, 0:L], k.ones[:], tmp(t % 2), start=(t == 0),
                          stop=(t == KT - 1)).then_inc(added, 1)

        @block.vector
        def _(dve):
            dve.wait_ge(meaned, 1)
            for t in range(KT):
                dve.tensor_tensor(x(t), x(t), mean, ALU.subtract).then_inc(centred, 1)
            for t in range(KT):
                dve.wait_ge(centred, t + 1)
                if t >= 2:
                    dve.wait_ge(added, t - 1)
                dve.tensor_tensor(tmp(t % 2), x(t), x(t), ALU.mult).then_inc(squared, 1)
            dve.wait_ge(root, 1)
            dve.reciprocal(k.rstd[:, 0:L], k.rstd[:, 0:L]).then_inc(inverse, 1)
            dve.wait_ge(inverse, 1)
            for t in range(KT):
                dve.tensor_tensor(x(t), x(t), k.rstd[:, 0:L], ALU.mult).then_inc(scaled, 1)

        @block.scalar
        def _(act):
            act.wait_ge(summed, 1)
            act.mul(mean, k.ps[1][:, 0:L], 1.0 / D).then_inc(meaned, 1)
            act.wait_ge(added, KT)
            act.activation(k.rstd[:, 0:L], k.ps[0][:, 0:L], ACT.Sqrt, bias=k.eps[:, 0:1],
                           scale=1.0 / D).then_inc(root, 1)
            for t in range(KT):
                act.wait_ge(scaled, t + 1)
                act.activation(x(t), x(t), ACT.Silu, bias=k.col("ln_b")[:, t:t + 1],
                               scale=k.col("ln_g")[:, t:t + 1]).then_inc(written, 1)


def channel_norm(k, name, tile, tiles, per_sum, n, scale, bias, tmp0, before=None, after=None):
    nc = k.nc
    tmp = lambda r: k.t(tmp0 + 2 * r, 2).rearrange("p s c -> p (s c)")[:, 0:n]
    sums = 4 // per_sum
    bank = (lambda r: k.ps[r]) if per_sum == 1 else (lambda r: k.ps[0])
    nafter = 2 if after is not None else 1
    with ExitStack() as stage:
        sem = lambda s: k.sem(stage, f"{name}_{s}")
        activated, squared, summed, root, inverse, scaled = (sem(s) for s in (
            "activated", "squared", "summed", "root", "inverse", "scaled"))
        block = stage.enter_context(nc.Block())

        @block.vector
        def _(dve):
            with dve.Fori(0, tiles // 4) as g:
                for r in range(4):
                    if before is not None:
                        dve.wait_ge(activated, g * 4 + (r + 1))
                    dve.tensor_tensor(tmp(r), tile(g * 4 + r), tile(g * 4 + r), ALU.mult).then_inc(squared, 1)
                for r in range(sums):
                    dve.wait_ge(root, g * sums + (r + 1))
                    dve.reciprocal(tmp(r), tmp(r)).then_inc(inverse, 1)
                for r in range(4):
                    dve.wait_ge(inverse, g * sums + (r // per_sum + 1))
                    dve.tensor_tensor(tile(g * 4 + r), tile(g * 4 + r), tmp(r // per_sum),
                                      ALU.mult).then_inc(scaled, 1)
                if after is not None:
                    for r in range(4):
                        dve.wait_ge(scaled, g * (4 * nafter) + (r + 1))
                        after(dve, g * 4 + r).then_inc(scaled, 1)
                dve.wait_ge(scaled, (g * 4 + 4) * nafter)

        @block.tensor
        def _(pe):
            with pe.Fori(0, tiles // 4) as g:
                for r in range(4):
                    pe.wait_ge(squared, g * 4 + (r + 1))
                    mm = pe.matmul(bank(r)[:, 0:n], k.ones[:], tmp(r), start=(r % per_sum == 0),
                                   stop=(r % per_sum == per_sum - 1))
                    if r % per_sum == per_sum - 1:
                        mm.then_inc(summed, 1)

        @block.scalar
        def _(act):
            with act.Fori(0, tiles // 4) as g:
                if before is not None:
                    for r in range(4):
                        act.activation(tile(g * 4 + r), tile(g * 4 + r), before).then_inc(activated, 1)
                for r in range(sums):
                    act.wait_ge(summed, g * sums + (r + 1))
                    act.activation(tmp(r), bank(r * per_sum)[:, 0:n], ACT.Sqrt, bias=bias,
                                   scale=scale).then_inc(root, 1)


def delta_gates(k):
    nc = k.nc
    ab = k.t(184, 2).rearrange("p s c -> p (s c)")
    z1 = k.t(186, 2).rearrange("p s c -> p (s c)")
    z2 = k.t(188, 2).rearrange("p s c -> p (s c)")
    tri = k.t(190, 1).rearrange("p s (m c) -> p (s m) c", m=2)
    w = k.t(180, 4).rearrange("p s c -> p (s c)").rearrange("p (t c) -> p t c", c=64)
    with ExitStack() as stage:
        sem = lambda s: k.sem(stage, f"gates_{s}")
        wab_in, product, act_step, dve_step, turned, cums = (sem(s) for s in (
            "weights_in", "product", "act_step", "dve_step", "turned", "sums"))
        block = stage.enter_context(nc.Block())

        @block.sync
        def _(sp):
            sp.dma_start(k.t(180, 4).rearrange("p s c -> p (s c)"), k.i["w_ab"]).then_inc(wab_in, 16)
            sp.dma_start(k.t(190, 1)[:, 0, :], k.i["cst"][:, 256 + 14 * P:256 + 16 * P]).then_inc(wab_in, 16)

        @block.tensor
        def _(pe):
            pe.wait_ge(wab_in, 32)
            for kt in range(KT):
                mm = pe.matmul(k.out(0, 2 * L)[0:64], w[:, kt, :], k.hx(kt), start=(kt == 0), stop=(kt == KT - 1))
            mm.then_inc(product, 1)
            pe.wait_ge(dve_step, 4)
            for c in range(4):
                mm = pe.transpose(k.ps[1][:, 64 * c:64 * c + 64], ab[0:64, P * c:P * c + P], k.ident[0:64, 0:64])
            mm.then_inc(turned, 1)
            pe.wait_ge(dve_step, 5)
            for c in range(4):
                for d in range(2):
                    pe.matmul(k.ps[2][:, 32 * c + 16 * d:32 * c + 16 * d + 16], tri[:, d, :],
                              k.gb[:, c, 16 * d:16 * d + 16], start=True, stop=True)
            for c in range(4):
                mm = pe.matmul(k.ps[3][:, 32 * c:32 * c + 32], k.ones[:], k.gb[:, c, 0:32], start=True, stop=True)
            mm.then_inc(cums, 1)

        @block.scalar
        def _(act):
            act.wait_ge(product, 1)
            act.activation(ab[32:64, :], k.ps[0][32:64, :], ACT.Sigmoid).then_inc(act_step, 1)
            act.activation(k.neg_a[0:32, :], k.col("dn_alog")[0:32, :], ACT.Exp).then_inc(act_step, 1)
            act.wait_ge(dve_step, 1)
            act.activation(z2[0:32, :], z1[0:32, :], ACT.Abs).then_inc(act_step, 1)
            act.wait_ge(act_step, 3)
            act.activation(z2[0:32, :], z2[0:32, :], ACT.Exp, scale=-1.0).then_inc(act_step, 1)
            act.wait_ge(act_step, 4)
            act.activation(z2[0:32, :], z2[0:32, :], ACT.Ln, bias=1.0).then_inc(act_step, 1)
            act.wait_ge(dve_step, 8)
            act.activation(k.kdec, k.kdec, ACT.Exp).then_inc(act_step, 1)
            act.activation(k.etot, k.etot, ACT.Exp).then_inc(act_step, 1)
            act.activation(k.negegc, k.gsum, ACT.Exp).then_inc(act_step, 1)

        @block.vector
        def _(dve):
            dve.wait_ge(act_step, 2)
            dve.tensor_scalar(z1[0:32, :], k.ps[0][0:32, :], k.col("dn_dtb")[0:32, :], None,
                              ALU.add).then_inc(dve_step, 1)
            dve.tensor_scalar(k.neg_a[0:32, :], k.neg_a[0:32, :], -1.0, None, ALU.mult).then_inc(dve_step, 1)
            dve.wait_ge(act_step, 5)
            dve.wait_ge(dve_step, 2)
            dve.scalar_tensor_tensor(out=z1[0:32, :], in0=z1[0:32, :], scalar=0.0, in1=z2[0:32, :],
                                     op0=ALU.max, op1=ALU.add).then_inc(dve_step, 1)
            dve.wait_ge(dve_step, 3)
            dve.tensor_scalar(ab[0:32, :], z1[0:32, :], k.neg_a[0:32, :], None, ALU.mult).then_inc(dve_step, 1)
            dve.wait_ge(turned, 1)
            dve.tensor_copy(k.gb, k.ps[1][:, 0:256].rearrange("p (c r) -> p c r", c=4)).then_inc(dve_step, 1)
            dve.wait_ge(cums, 1)
            dve.tensor_copy(k.gsum, k.ps[2][:, 0:P]).then_inc(dve_step, 1)
            dve.tensor_copy(k.etot, k.ps[3][:, 0:P]).then_inc(dve_step, 1)
            dve.wait_ge(dve_step, 7)
            dve.tensor_tensor(k.kdec, k.etot, k.gsum, ALU.subtract).then_inc(dve_step, 1)
            dve.wait_ge(act_step, 8)
            dve.tensor_scalar(k.negegc, k.negegc, -1.0, None, ALU.mult).then_inc(dve_step, 1)


def gated_delta(k):
    nc = k.nc
    C = 4
    LEVELS = 7
    ORDER = ((2, 3, 0, 1), (3, 2, 1, 0))
    cur = [48]

    def take(slots):
        if cur[0] <= 64 and cur[0] + slots > 64:
            cur[0] = 144
        if 144 <= cur[0] <= 160 and cur[0] + slots > 160:
            cur[0] = 176
        cur[0] += slots
        assert cur[0] <= 195
        return k.t(cur[0] - slots, slots).rearrange("p s c -> p (s c)")

    masks = take(8).rearrange("p (m c) -> p m c", c=P)
    level = lambda d, l: masks[:, 7 * d + l, :].unsqueeze(1).broadcast_to([P, C, P])
    incl = lambda d: masks[:, 14 + d, :].unsqueeze(1).broadcast_to([P, C, P])
    four = lambda ap: ap.rearrange("p (c t) -> p c t", t=P)
    kst, vst, vtok = four(take(2)), four(take(2)), four(take(2))
    qst = four(take(1))
    e = [four(take(2)) for d in range(2)]
    n_ = [four(take(2)) for d in range(2)]
    nl = [four(take(2)) for d in range(2)]
    inv = [four(take(2)) for d in range(2)]
    invt = [four(take(2)) for d in range(2)]
    ksc = [four(take(2)) for d in range(2)]
    attn = [four(take(1)) for d in range(2)]
    qg = [four(take(1)) for d in range(2)]
    ost = [four(take(1)) for d in range(2)]
    rs = [four(take(1)) for d in range(2)]
    r0 = [rs[d][:, 0, :] for d in range(2)]
    state = [rs[d][:, 1, :] for d in range(2)]
    vn = k.t(195, 2).rearrange("p s (d t) -> p (s d) t", t=P)
    gst = k.gst
    ident4 = k.ident[:].unsqueeze(1).broadcast_to([P, C, P])
    bX, bY, bZ, bS = (4, 5), (0, 2), (1, 3), (6, 7)
    bank = lambda b: k.ps[b][:].rearrange("p (c t) -> p c t", t=P)

    with ExitStack() as stage:
        sem = lambda s: k.sem(stage, f"dn_{s}")
        sem2 = lambda s: [sem(f"{s}{d}") for d in range(2)]
        masks_in, k_staged, v_staged, q_staged, g_staged = (sem(s) for s in (
            "masks_in", "k_staged", "v_staged", "q_staged", "g_staged"))
        kk_ready, ktok_ready, vtok_ready, ksc_done, vtok_done, head_done = (sem(s) for s in (
            "kk_ready", "ktok_ready", "vtok_ready", "ksc_done", "vtok_done", "head_done"))
        grow_ready, eg_done, diff_done, e_done, em_done, n_done, attn_done, qg_done = (sem2(s) for s in (
            "grow_ready", "eg_done", "diff_done", "e_done", "em_done", "n_done", "attn_done", "qg_done"))
        nl_done, invt_done, inv_done, turned, x_ready, x_copied, y_ready, yt_ready = (sem2(s) for s in (
            "nl_done", "invt_done", "inv_done", "turned", "x_ready", "x_copied", "y_ready", "yt_ready"))
        ks_ready, r0_done, new_ready, vn_done, o_ready, snew_ready, s_done, o_kept = (sem2(s) for s in (
            "ks_ready", "r0_done", "new_ready", "vn_done", "o_ready", "snew_ready", "s_done", "o_kept"))
        block = stage.enter_context(nc.Block())

        def percol(ap, h, c, d):
            return ap[:, bass.ds(h + (32 * c + 16 * d), 1)]

        def beta(h, c, d):
            return k.gb.rearrange("p c r -> p (c r)")[:, bass.ds(h + (64 * c + 32 + 16 * d), 1)]

        def heads(eng, body):
            body(0, True)
            with eng.Fori(1, HEADS) as h:
                eng.wait_ge(head_done, h)
                body(h, False)

        @block.sync
        def _(sp):
            sp.dma_start(masks.rearrange("p m c -> p (m c)"), k.i["cst"][:, 256:256 + 16 * P]).then_inc(masks_in, 16)

        @block.tensor
        def _(pe):
            pe.wait_ge(masks_in, 16)

            def body(h, first):
                pe.wait_ge(k_staged, h + 1)
                for c in range(C):
                    pe.matmul(bank(0)[:, c, :], kst[:, c, :], kst[:, c, :], start=True, stop=True)
                pe.wait_ge(q_staged, h + 1)
                for c in range(2):
                    mm = pe.matmul(bank(1)[:, c, :], kst[:, c, :], qst[:, c, :], start=True, stop=True)
                mm.then_inc(kk_ready, 1)
                pe.wait_ge(g_staged, h + 1)
                for d in range(2):
                    for c in range(C):
                        mm = pe.matmul(bank(bX[d])[:, c, :], gst[:, c, d:d + 1].broadcast_to([P, P]),
                                       masks[:, 14 + d, :], start=True, stop=True)
                    mm.then_inc(grow_ready[d], 1)
                for c in range(C):
                    mm = pe.transpose(bank(2)[:, c, :], kst[:, c, :], k.ident[:])
                mm.then_inc(ktok_ready, 1)
                pe.wait_ge(v_staged, h + 1)
                for c in range(C):
                    mm = pe.transpose(bank(3)[:, c, :], vst[:, c, :], k.ident[:])
                mm.then_inc(vtok_ready, 1)
                for d in range(2):
                    pe.wait_ge(nl_done[d], h * LEVELS + 1)
                    for c in range(C):
                        mm = pe.transpose(bank(bX[d])[:, c, :], nl[d][:, c, :], k.ident[:])
                    mm.then_inc(turned[d], 1)
                pe.wait_ge(n_done[0], h + 1)
                pe.wait_ge(n_done[1], h + 1)
                pe.wait_ge(attn_done[1], h + 1)
                pe.wait_ge(ksc_done, h + 1)
                pe.wait_ge(vtok_done, h + 1)
                for l in range(1, LEVELS):
                    for d in range(2):
                        pe.wait_ge(nl_done[d], h * LEVELS + (l + 1))
                        pe.wait_ge(inv_done[d], h * (LEVELS - 1) + l)
                        for c in range(C):
                            mm = pe.matmul(bank(bX[d])[:, c, :], nl[d][:, c, :], inv[d][:, c, :], start=True, stop=True)
                        mm.then_inc(x_ready[d], 1)
                    for d in range(2):
                        pe.wait_ge(x_copied[d], h * (LEVELS - 1) + l)
                        pe.wait_ge(invt_done[d], h * LEVELS + l)
                        if l < LEVELS - 1:
                            for c in range(C):
                                mm = pe.matmul(bank(bY[d])[:, c, :], invt[d][:, c, :], e[d][:, c, :], start=True, stop=True)
                            mm.then_inc(y_ready[d], 1)
                        for c in range(C):
                            mm = pe.matmul(bank(bZ[d])[:, c, :], e[d][:, c, :], invt[d][:, c, :], start=True, stop=True)
                        mm.then_inc(yt_ready[d], 1)
                for s in range(C):
                    if s > 0:
                        for d in range(2):
                            c = ORDER[d][s]
                            pe.wait_ge(s_done[d], h * 3 + s)
                            pe.matmul(bank(bS[d])[:, 0, :], kst[:, c, :], state[d], start=True,
                                      stop=True).then_inc(ks_ready[d], 1)
                    for d in range(2):
                        c = ORDER[d][s]
                        if s == 0:
                            pe.wait_ge(invt_done[d], h * LEVELS + LEVELS)
                            rhs = vtok[:, c, :]
                        else:
                            pe.wait_ge(r0_done[d], h * 3 + s)
                            rhs = r0[d]
                        pe.matmul(bank(bS[d])[:, 1, :], invt[d][:, c, :], rhs, start=True,
                                  stop=True).then_inc(new_ready[d], 1)
                    for d in range(2):
                        c = ORDER[d][s]
                        pe.wait_ge(vn_done[d], h * 4 + (s + 1))
                        if s >= 2:
                            if s == 2:
                                pe.wait_ge(qg_done[d], h + 1)
                            pe.matmul(bank(bS[d])[:, 3, :], state[d], qg[d][:, c, :], start=True, stop=False)
                            pe.matmul(bank(bS[d])[:, 3, :], vn[:, d, :], attn[d][:, c, :], start=False,
                                      stop=True).then_inc(o_ready[d], 1)
                        if s < 3:
                            pe.matmul(bank(bS[d])[:, 2, :], ksc[d][:, c, :], vn[:, d, :], start=True,
                                      stop=True).then_inc(snew_ready[d], 1)

            heads(pe, body)

        @block.scalar
        def _(act):
            act.wait_ge(masks_in, 16)

            def body(h, first):
                act.copy(kst.rearrange("p c t -> p (c t)"), k.key_tile(h)).then_inc(k_staged, 1)
                for d in range(2):
                    act.wait_ge(grow_ready[d], h + 1)
                    act.activation(qg[d], bank(bX[d])[:, 0:2, :], ACT.Exp).then_inc(eg_done[d], 1)
                for d in range(2):
                    act.wait_ge(diff_done[d], h + 1)
                    act.activation(e[d], e[d], ACT.Exp).then_inc(e_done[d], 1)
                act.wait_ge(ktok_ready, h + 1)
                for d in range(2):
                    for c in range(C):
                        ins = act.activation(ksc[d][:, c, :], bank(2)[:, c, :], ACT.Copy,
                                             scale=percol(k.kdec, h, c, d))
                ins.then_inc(ksc_done, 1)
                act.wait_ge(vtok_ready, h + 1)
                act.copy(vtok, bank(3)).then_inc(vtok_done, 1)
                for l in range(1, LEVELS):
                    for d in range(2):
                        act.wait_ge(x_ready[d], h * (LEVELS - 1) + l)
                        if l == 1:
                            act.wait_ge(attn_done[d], h + 1)
                        else:
                            act.wait_ge(yt_ready[d], h * (LEVELS - 1) + (l - 1))
                        act.copy(e[d], bank(bX[d])).then_inc(x_copied[d], 1)
                for s in range(C):
                    for d in range(2):
                        act.wait_ge(new_ready[d], h * 4 + (s + 1))
                        if s > 0:
                            act.wait_ge(snew_ready[d], h * 3 + s)
                        act.activation(vn[:, d, :], bank(bS[d])[:, 1, :], ACT.Copy,
                                       scale=beta(h, ORDER[d][s], d)).then_inc(vn_done[d], 1)

            heads(act, body)

        @block.gpsimd
        def _(pool):
            pool.wait_ge(masks_in, 16)

            def body(h, first):
                pool.tensor_copy(gst, k.gb[:, :, 0:32].rearrange("p c (d n) -> p c d n", d=2)[
                    :, :, :, bass.ds(h, 1)].rearrange("p c d n -> p c (d n)")).then_inc(g_staged, 1)
                pool.tensor_copy(vst.rearrange("p c t -> p (c t)"), k.value_tile(h)).then_inc(v_staged, 1)
                for d in range(2):
                    pool.wait_ge(e_done[d], h + 1)
                    pool.tensor_tensor(e[d], e[d], incl(d), ALU.mult).then_inc(em_done[d], 1)
                for l in range(LEVELS):
                    for d in range(2):
                        if l == 0:
                            pool.wait_ge(n_done[d], h + 1)
                        elif l == 1:
                            pool.wait_ge(turned[d], h + 1)
                            pool.wait_ge(invt_done[d], h * LEVELS + 1)
                        else:
                            pool.wait_ge(x_ready[d], h * (LEVELS - 1) + (l - 1))
                        pool.tensor_tensor(nl[d], n_[d], level(d, l), ALU.mult).then_inc(nl_done[d], 1)

            heads(pool, body)

        @block.vector
        def _(dve):
            dve.wait_ge(masks_in, 16)

            def body(h, first):
                dve.tensor_copy(qst.rearrange("p c t -> p (c t)"), k.query_tile(h)).then_inc(q_staged, 1)
                for d in range(2):
                    dve.wait_ge(eg_done[d], h + 1)
                    for c in range(C):
                        ins = dve.tensor_scalar(e[d][:, c, :], bank(bX[d])[:, c, :], percol(k.gsum, h, c, d), 0.0,
                                                ALU.subtract, ALU.min)
                    ins.then_inc(diff_done[d], 1)
                for d in range(2):
                    dve.wait_ge(q_staged, h + 1)
                    dve.tensor_tensor(qg[d], qg[d], qst, ALU.mult).then_inc(qg_done[d], 1)
                dve.wait_ge(kk_ready, h + 1)
                for d in range(2):
                    dve.wait_ge(em_done[d], h + 1)
                    for c in range(C):
                        ins = dve.scalar_tensor_tensor(out=n_[d][:, c, :], in0=bank(0)[:, c, :],
                                                       scalar=beta(h, c, d), in1=e[d][:, c, :],
                                                       op0=ALU.mult, op1=ALU.mult)
                    ins.then_inc(n_done[d], 1)
                    dve.tensor_tensor(attn[d], bank(1)[:, 0:2, :], e[d][:, 0:2, :], ALU.mult).then_inc(attn_done[d], 1)
                for d in range(2):
                    dve.wait_ge(nl_done[d], h * LEVELS + 1)
                    dve.tensor_tensor(invt[d], ident4, nl[d], ALU.subtract).then_inc(invt_done[d], 1)
                    dve.wait_ge(turned[d], h + 1)
                    dve.tensor_tensor(inv[d], ident4, bank(bX[d]), ALU.subtract).then_inc(inv_done[d], 1)
                for l in range(1, LEVELS):
                    for d in range(2):
                        if l < LEVELS - 1:
                            dve.wait_ge(y_ready[d], h * (LEVELS - 2) + l)
                            dve.wait_ge(inv_done[d], h * (LEVELS - 1) + l)
                            dve.tensor_tensor(inv[d], inv[d], bank(bY[d]), ALU.subtract).then_inc(inv_done[d], 1)
                        dve.wait_ge(yt_ready[d], h * (LEVELS - 1) + l)
                        dve.wait_ge(invt_done[d], h * LEVELS + l)
                        dve.tensor_tensor(invt[d], invt[d], bank(bZ[d]), ALU.subtract).then_inc(invt_done[d], 1)
                for s in range(C):
                    for d in range(2):
                        c = ORDER[d][s]
                        if s > 0:
                            dve.wait_ge(ks_ready[d], h * 3 + s)
                            if s == 1:
                                dve.wait_ge(vtok_done, h + 1)
                            dve.scalar_tensor_tensor(out=r0[d], in0=bank(bS[d])[:, 0, :],
                                                     scalar=percol(k.negegc, h, c, d), in1=vtok[:, c, :],
                                                     op0=ALU.mult, op1=ALU.add).then_inc(r0_done[d], 1)
                    for d in range(2):
                        c = ORDER[d][s]
                        if s < 3:
                            dve.wait_ge(snew_ready[d], h * 3 + (s + 1))
                        if s >= 2:
                            dve.wait_ge(o_ready[d], h * 2 + (s - 1))
                            dve.tensor_copy(ost[d][:, c, :], bank(bS[d])[:, 3, :]).then_inc(o_kept[d], 1)
                        if s == 0:
                            dve.tensor_copy(state[d], bank(bS[d])[:, 2, :]).then_inc(s_done[d], 1)
                        elif s < 3:
                            dve.wait_ge(s_done[d], h * 3 + s)
                            dve.scalar_tensor_tensor(out=state[d], in0=state[d], scalar=percol(k.etot, h, c, d),
                                                     in1=bank(bS[d])[:, 2, :], op0=ALU.mult,
                                                     op1=ALU.add).then_inc(s_done[d], 1)
                dve.wait_ge(o_kept[0], h * 2 + 2)
                dve.wait_ge(o_kept[1], h * 2 + 2)
                dve.tensor_tensor(k.query_tile(h), ost[0].rearrange("p c t -> p (c t)"),
                                  ost[1].rearrange("p c t -> p (c t)"), ALU.add).then_inc(head_done, 1)

            heads(dve, body)


def elementwise(k, name, ops):
    with ExitStack() as stage:
        finished = k.sem(stage, f"{name}_finished")
        block = stage.enter_context(k.nc.Block())

        @block.vector
        def _(dve):
            for op in ops:
                op(dve).then_inc(finished, 1)


PEER_HEADS = 8
TOPK = 16


def peer_scores(k, q_slot, key_slot, out_slot):
    nc = k.nc
    with ExitStack() as stage:
        keys_in, scored, copied = (k.sem(stage, s) for s in (
            "peer_keys_in", "peer_scored", "peer_scores_copied"))
        block = stage.enter_context(nc.Block())
        keys = k.t(key_slot, 8).rearrange("p s c -> p (s c)").rearrange("p (f h n) -> p f h n", f=2, h=PEER_HEADS)
        out = k.t(out_slot, 16).rearrange("p s c -> p (s c)").rearrange("p (b c) -> p b c", c=512)

        @block.sync
        def _(sp):
            sp.dma_start(k.t(key_slot, 8).rearrange("p s c -> p (s c)"), k.i["peer_keys"]).then_inc(keys_in, 16)
            sp.dma_start(k.iota, k.i["cst"][:, 256 + 16 * P:256 + 17 * P]).then_inc(keys_in, 16)

        @block.tensor
        def _(pe):
            pe.wait_ge(keys_in, 32)
            for b in range(8):
                tt, hp = b // 4, b % 4
                for m in range(4):
                    h, f = 2 * hp + m // 2, m % 2
                    mm = pe.matmul(k.ps[b][:, m * P:(m + 1) * P],
                                   k.t(q_slot + 2 * h + f, 1)[:, 0, tt * P:(tt + 1) * P],
                                   keys[:, f, h, :], start=True, stop=True)
                mm.then_inc(scored, 1)

        @block.scalar
        def _(act):
            for b in range(8):
                act.wait_ge(scored, b + 1)
                act.copy(out[:, b, :], k.ps[b][:]).then_inc(copied, 1)


def peer_select_side(k, score_slot):
    out = {}

    def sems(stage):
        for n in ("step", "tail", "exp_ready"):
            out[n] = k.sem(stage, f"peer_select_{n}")

    row = lambda slot: k.t(slot, 1)[:, 0, :]
    halves = row(192).rearrange("p (f n) -> p f n", f=2)
    cand, eq, small = row(193), row(194), row(196)
    value = small[:, 0:32].rearrange("p (f n) -> p f n", f=2)
    index = small[:, 32:64].bitcast(U32).rearrange("p (f n) -> p f n", f=2)
    indexf = small[:, 64:96].rearrange("p (f n) -> p f n", f=2)
    best = small[:, 96:112]
    pos = small[:, 112:128].bitcast(U32)
    part = small[:, 128:160].bitcast(U32).rearrange("p (f n) -> p f n", f=2)
    partf = small[:, 160:192].rearrange("p (f n) -> p f n", f=2)
    top, total = small[:, 192:208], small[:, 208:224]
    scores = k.t(score_slot, 16).rearrange("p s c -> p (s c)")
    eq3 = eq.rearrange("p (j a) -> p j a", a=TOPK)

    def vector(dve):
        def top16(values, v, ix, done):
            done(dve.max(out=v[:, 0:8], in_=values))
            done(dve.max_index(out=ix[:, 0:8], in_max=v[:, 0:8], in_values=values))
            done(dve.match_replace(out=values, in_to_replace=v[:, 0:8], in_values=values, imm_value=NEG))
            done(dve.max(out=v[:, 8:16], in_=values))
            done(dve.max_index(out=ix[:, 8:16], in_max=v[:, 8:16], in_values=values))

        with dve.Fori(0, 2 * PEER_HEADS) as u:
            n = [0]

            def done(ins):
                n[0] += 1
                ins.then_inc(out["step"], 1)
                dve.wait_ge(out["step"], n[0])

            done(dve.tensor_copy(row(192), scores[:, bass.ds(u * 256, 256)]))
            for f in range(2):
                top16(halves[:, f, :], value[:, f, :], index[:, f, :], done)
            done(dve.tensor_copy(indexf, index))
            done(dve.tensor_tensor(cand.rearrange("p (a b) -> p a b", b=TOPK),
                                   value[:, 0, :].unsqueeze(2).broadcast_to([P, TOPK, TOPK]),
                                   value[:, 1, :].unsqueeze(1).broadcast_to([P, TOPK, TOPK]), ALU.add))
            top16(cand, best, pos, done)
            done(dve.tensor_scalar(part[:, 0, :], pos, 4, None, ALU.logical_shift_right))
            done(dve.tensor_scalar(part[:, 1, :], pos, 15, None, ALU.bitwise_and))
            done(dve.tensor_copy(partf, part))
            for f in range(2):
                done(dve.tensor_tensor(eq3, partf[:, f, :].unsqueeze(2).broadcast_to([P, TOPK, TOPK]),
                                       k.iota[:, 0:TOPK].unsqueeze(1).broadcast_to([P, TOPK, TOPK]), ALU.is_equal))
                done(dve.tensor_tensor(eq3, eq3, indexf[:, f, :].unsqueeze(1).broadcast_to([P, TOPK, TOPK]), ALU.mult))
                done(dve.tensor_reduce(row(197 + f)[:, bass.ds(u * TOPK, TOPK)], eq3, AX.X, ALU.add))
            done(dve.tensor_copy(row(199)[:, bass.ds(u * TOPK, TOPK)], best))
            dve.sem_clear(out["step"])
        w = row(199).rearrange("p (u j) -> p u j", j=TOPK)
        dve.tensor_tensor(eq3, w, w[:, :, 0:1].broadcast_to([P, 16, TOPK]), ALU.subtract).then_inc(out["tail"], 1)
        dve.wait_ge(out["exp_ready"], 1)
        dve.tensor_reduce(total, w, AX.X, ALU.add).then_inc(out["tail"], 1)
        dve.wait_ge(out["tail"], 2)
        dve.reciprocal(total, total).then_inc(out["tail"], 1)
        dve.wait_ge(out["tail"], 3)
        dve.tensor_tensor(w, w, total.unsqueeze(2).broadcast_to([P, 16, TOPK]), ALU.mult).then_inc(out["tail"], 1)

    def scalar(act):
        act.wait_ge(out["tail"], 1)
        act.activation(row(199), eq, ACT.Exp).then_inc(out["exp_ready"], 1)

    return {"sems": sems, "vector": vector, "scalar": scalar}


def peer_weights(k, act_slot):
    nc = k.nc
    G = 4
    row = lambda slot: k.t(slot, 1)[:, 0, :]
    i1t, i2t, wt = row(192), row(193), row(194)
    hot = k.t(24, 8).rearrange("p (b m s) c -> p b m (s c)", b=2, m=2)
    hot = [[hot[:, b, m, :].rearrange("p (t n) -> p t n", t=G) for m in range(2)] for b in range(2)]
    acts = k.t(act_slot, P)
    with ExitStack() as stage:
        sem = lambda s: k.sem(stage, f"peer_{s}")
        turned, columns, hot1, apart, far, hot2, placed, applied = (sem(s) for s in (
            "turned", "columns_ready", "hot1_ready", "distances", "absolute", "hot2_ready", "weights_placed",
            "weights_applied"))
        block = stage.enter_context(nc.Block())

        @block.tensor
        def _(pe):
            for m in range(3):
                for tt in range(2):
                    mm = pe.transpose(k.ps[m][:, tt * P:(tt + 1) * P], row(197 + m)[:, tt * P:(tt + 1) * P], k.ident[:])
                mm.then_inc(turned, 1)
            pe.wait_ge(columns, 3)

            def pair(g, first):
                for b in range(2):
                    pe.wait_ge(hot1, g * 2 + (b + 1))
                    pe.wait_ge(hot2, g * 2 + (b + 1))
                    if not first:
                        pe.wait_ge(applied, g * 2 + (b - 1))
                    for t in range(G):
                        mm = pe.matmul(k.ps[b][:, t * P:(t + 1) * P], hot[b][1][:, t, :], hot[b][0][:, t, :],
                                       start=True, stop=True)
                    mm.then_inc(placed, 1)

            pair(0, True)
            with pe.Fori(1, L // G // 2) as g:
                pair(g, False)

        @block.scalar
        def _(act):
            for m, dst in enumerate((i1t, i2t, wt)):
                act.wait_ge(turned, m + 1)
                act.copy(dst, k.ps[m][:, 0:L]).then_inc(columns, 1)
            with act.Fori(0, L // G // 2) as g:
                for b in range(2):
                    act.wait_ge(apart, g * 2 + (b + 1))
                    act.activation(hot[b][1], hot[b][1], ACT.Abs).then_inc(far, 1)
                    act.wait_ge(far, g * 2 + (b + 1))
                    act.activation(hot[b][1], hot[b][1], ACT.Relu, scale=-1.0, bias=1.0).then_inc(hot2, 1)

        @block.vector
        def _(dve):
            dve.wait_ge(columns, 3)

            def one_hot(g, b):
                for t in range(G):
                    tok = bass.ds(g * (2 * G) + (b * G + t), 1)
                    ins = dve.tensor_scalar(hot[b][0][:, t, :], k.iota, i1t[:, tok], wt[:, tok],
                                            ALU.is_equal, ALU.mult)
                ins.then_inc(hot1, 1)

            def apply(g, b):
                dve.wait_ge(placed, g * 2 + (b + 1))
                a = acts[:, :, bass.ds(g * (2 * G) + b * G, G)].rearrange("p n t -> p t n")
                dve.tensor_tensor(a, a, k.ps[b][:].rearrange("p (t n) -> p t n", t=G), ALU.mult).then_inc(applied, 1)

            one_hot(0, 0)
            one_hot(0, 1)
            with dve.Fori(0, L // G // 2 - 1) as g:
                for b in range(2):
                    apply(g, b)
                    one_hot(g + 1, b)
            for b in range(2):
                apply(L // G // 2 - 1, b)

        @block.gpsimd
        def _(pool):
            pool.wait_ge(columns, 3)

            def pair(g, first):
                for b in range(2):
                    if not first:
                        pool.wait_ge(placed, g * 2 + (b - 1))
                    tok = bass.ds(g * (2 * G) + b * G, G)
                    pool.tensor_tensor(hot[b][1], k.iota.unsqueeze(1).broadcast_to([P, G, P]),
                                       i2t[:, tok].unsqueeze(2).broadcast_to([P, G, P]),
                                       ALU.subtract).then_inc(apart, 1)

            pair(0, True)
            with pool.Fori(1, L // G // 2) as g:
                pair(g, False)


def expert_output(k, v, act_slot, x_slot, gate, x_saved, following3):
    nc = k.nc
    s = k.raws
    tiles = v.shape[0]
    groups = tiles // SLOTS
    acts = k.t(act_slot, tiles)
    part = lambda m, r: k.r(196 + 2 * m + r % 2, 1)[:, 0, :]
    with ExitStack() as stage:
        added, a_high, a_low, x_in = (k.sem(stage, f"expert_{n}") for n in ("added", "acts_high", "acts_low", "x_in"))
        block = stage.enter_context(nc.Block())

        @block.sync
        def _(sp):
            sp.dma_start(k.t(x_slot, KT), x_saved).then_inc(x_in, 16)
            load_raw(k, sp, v, tiles, s)
            load_next(k, sp, None, following3, s + tiles)

        @block.tensor
        def _(pe):
            def group(g, first, last):
                for r in range(SLOTS):
                    pe.wait_ge(a_low, g * SLOTS + (r + 1))
                    for q in range(2):
                        pe.wait_ge(k.lo_done, g * (2 * SLOTS) + (2 * (s + r) + q + 1))
                        for j in range(8):
                            m = 8 * q + j
                            vh, vl = (k.staged(p, q)[:, j * P:(j + 1) * P] for p in range(2))
                            out = k.ps[m // 2][:, (m % 2) * L:(m % 2 + 1) * L]
                            fresh = first and r == 0 and m % 2 == 0
                            pe.matmul(out, vh, part(0, r), start=fresh, stop=False, skip_group_check=True)
                            pe.matmul(out, vh, part(1, r), start=False, stop=False, skip_group_check=True)
                            mm = pe.matmul(out, vl, part(0, r), start=False, stop=(last and r == SLOTS - 1),
                                           skip_group_check=True)
                        mm.then_inc(k.half_done, 1)

            group(0, True, False)
            with pe.Fori(1, groups - 1) as g:
                group(g, False, False)
            group(groups - 1, False, True)

        @block.scalar
        def _(act):
            def group(g, first):
                for r in range(SLOTS):
                    if not (first and r < 2):
                        act.wait_ge(k.half_done, g * (2 * SLOTS) + (2 * (s + r) - 2))
                    act.activation(part(0, r), flat(acts[:, bass.ds(g * SLOTS + r, 1), :]), ACT.Copy).then_inc(a_high, 1)
                    for q in range(2):
                        make_high(k, act, g, r, q, s, first)

            group(0, True)
            with act.Fori(1, groups) as g:
                group(g, False)

        @block.vector
        def _(dve):
            with dve.Fori(0, groups) as g:
                for r in range(SLOTS):
                    dve.wait_ge(a_high, g * SLOTS + (r + 1))
                    dve.tensor_tensor(part(1, r), flat(acts[:, bass.ds(g * SLOTS + r, 1), :]),
                                      part(0, r), ALU.subtract).then_inc(a_low, 1)
                    for q in range(2):
                        make_low(k, dve, g, r, q, s)
            dve.wait_ge(k.half_done, 2 * (s + tiles))
            dve.wait_ge(x_in, 16)
            for m in range(KT):
                x = k.t(x_slot + m, 1)[:, 0, :]
                dve.scalar_tensor_tensor(out=x, in0=k.ps[m // 2][:, (m % 2) * L:(m % 2 + 1) * L],
                                         scalar=gate[:, m:m + 1], in1=x, op0=ALU.mult, op1=ALU.add).then_inc(added, 1)

    k.raws += tiles


def save(k, name, slot, dram):
    with ExitStack() as stage:
        saved = k.sem(stage, f"{name}_saved")
        block = stage.enter_context(k.nc.Block())

        @block.sync
        def _(sp):
            sp.dma_start(dram, k.t(slot, KT)).then_inc(saved, 16)
            sp.wait_ge(saved, 16)


def dt_product(k, h_slot):
    H = 16
    with ExitStack() as stage:
        w_in, dt_ready, kept = (k.sem(stage, f"dt_{n}") for n in ("weights_in", "ready", "kept"))
        block = stage.enter_context(k.nc.Block())
        wdt = flat(k.t(80, 1))

        @block.sync
        def _(sp):
            sp.dma_start(wdt, k.i["w_dt"]).then_inc(w_in, 16)

        @block.tensor
        def _(pe):
            pe.wait_ge(w_in, 16)
            for kt in range(KT):
                mm = pe.matmul(k.ps[0][0:H, 0:L], wdt[:, kt * H:(kt + 1) * H], k.t(h_slot + kt, 1)[:, 0, :],
                               start=(kt == 0), stop=(kt == KT - 1))
            mm.then_inc(dt_ready, 1)

        @block.scalar
        def _(act):
            act.wait_ge(dt_ready, 1)
            act.copy(k.dt_raw[0:H, :], k.ps[0][0:H, 0:L]).then_inc(kept, 1)


def hgrn_decays(k, f_slot, work, key_slot, sum_slot):
    nc = k.nc
    f, t1, key, total = (flat(k.t(s, 8)) for s in (f_slot, work, key_slot, sum_slot))
    with ExitStack() as stage:
        a_step, v_step, ones_set = (k.sem(stage, f"hgrn_decay_{n}") for n in ("act", "dve", "ones"))
        block = stage.enter_context(nc.Block())
        one = flat(k.t(199, 1))

        @block.gpsimd
        def _(pool):
            pool.memset(one, 1.0).then_inc(ones_set, 1)

        @block.scalar
        def _(act):
            act.activation(t1, f, ACT.Abs).then_inc(a_step, 1)
            act.wait_ge(a_step, 1)
            act.activation(t1, t1, ACT.Exp, scale=-1.0).then_inc(a_step, 1)
            act.wait_ge(a_step, 2)
            act.activation(t1, t1, ACT.Ln, bias=1.0).then_inc(a_step, 1)
            act.wait_ge(v_step, 2)
            act.activation(key, key, ACT.Exp).then_inc(a_step, 1)

        @block.vector
        def _(dve):
            dve.wait_ge(a_step, 3)
            dve.scalar_tensor_tensor(out=t1, in0=f, scalar=0.0, in1=t1, op0=ALU.min, op1=ALU.subtract).then_inc(v_step, 1)
            dve.wait_ge(v_step, 1)
            dve.tensor_tensor(key, t1, f, ALU.subtract).then_inc(v_step, 1)
            dve.wait_ge(ones_set, 1)
            for h in range(8):
                dve.tensor_tensor_scan(total[:, h * L:(h + 1) * L], one, t1[:, h * L:(h + 1) * L], 0.0,
                                       ALU.mult, ALU.add).then_inc(v_step, 1)


def hgrn_attention(k, q_slot, v_slot, key_slot, sum_slot, out_slot, work):
    nc = k.nc
    H = 8
    q, key, total = flat(k.t(q_slot, 8)), flat(k.t(key_slot, 8)), flat(k.t(sum_slot, 8))
    vtok = flat(k.t(work, 8)).rearrange("p (t h c) -> p t h c", t=2, h=H)
    diag = flat(k.t(work + 8, 8)).rearrange("p (b c) -> p b c", c=512)
    off = flat(k.t(work + 16, 4)).rearrange("p (h c) -> p h c", h=H)
    e = flat(k.t(work + 20, 8))
    qk = flat(k.t(work + 28, 8))
    tmp = [flat(k.t(work + 36 + 2 * b, 2)) for b in range(2)]
    masks = flat(k.t(196, 4))[:, 0:7 * P].rearrange("p (m c) -> p m c", c=P)
    level_mask = lambda l: (k.ident if l < 0 else masks[:, l, :]).unsqueeze(1).broadcast_to([P, 4, P])
    v4 = lambda ap: ap.rearrange("p (b c) -> p b c", c=P)
    with ExitStack() as stage:
        sem = lambda s: k.sem(stage, f"hgrn_{s}")
        masks_in, turned, vtok_done, diff_done, e_done, qk_done, scored, masked, summed, off_ready, off_done, o_ready, o_done = (
            sem(s) for s in ("masks_in", "turned", "vtok_done", "diff_done", "e_done", "qk_done", "scored",
                             "masked", "summed", "off_ready", "off_done", "o_ready", "o_done"))
        block = stage.enter_context(nc.Block())

        @block.sync
        def _(sp):
            sp.dma_start(flat(k.t(196, 4))[:, 0:7 * P], k.i["cst"][:, 256:256 + 7 * P]).then_inc(masks_in, 16)

        @block.tensor
        def _(pe):
            for b in range(4):
                for m in range(4):
                    tt, h = (4 * b + m) // H, (4 * b + m) % H
                    mm = pe.transpose(k.ps[4 + b][:, m * P:(m + 1) * P],
                                      k.t(v_slot + h, 1)[:, 0, tt * P:(tt + 1) * P], k.ident[:])
                mm.then_inc(turned, 1)
            for n in range(8):
                if n:
                    pe.wait_ge(qk_done, 2 * n)
                for b in range(4):
                    if n:
                        pe.wait_ge(masked, 4 * (n - 1) + b + 1)
                    for m in range(4):
                        at = (4 * b + m) * P
                        lhs, rhs = (key, q) if n == 0 else (qk, qk)
                        mm = pe.matmul(k.ps[b][:, m * P:(m + 1) * P], lhs[:, at:at + P], rhs[:, at:at + P],
                                       start=True, stop=True)
                    mm.then_inc(scored, 1)
            pe.wait_ge(qk_done, 16)
            pe.wait_ge(vtok_done, 4)
            for b in range(2):
                for m in range(4):
                    h = 4 * b + m
                    mm = pe.matmul(k.ps[4 + b][:, m * P:(m + 1) * P], qk[:, h * L:h * L + P],
                                   qk[:, h * L + P:(h + 1) * L], start=True, stop=True)
                mm.then_inc(off_ready, 1)
            pe.wait_ge(off_done, 2)
            pe.wait_ge(summed, 28)
            for h in range(H):
                b = k.ps[h % 4]
                if h >= 4:
                    pe.wait_ge(o_done, h - 3)
                s = [diag[:, (2 * h + tt) // 4, ((2 * h + tt) % 4) * P:((2 * h + tt) % 4 + 1) * P] for tt in range(2)]
                pe.matmul(b[:, 0:P], vtok[:, 0, h, :], s[0], start=True, stop=True)
                pe.matmul(b[:, P:L], vtok[:, 0, h, :], off[:, h, :], start=True, stop=False)
                pe.matmul(b[:, P:L], vtok[:, 1, h, :], s[1], start=False, stop=True).then_inc(o_ready, 1)

        @block.scalar
        def _(act):
            for b in range(4):
                act.wait_ge(turned, b + 1)
                act.copy(flat(k.t(work + 2 * b, 2)), k.ps[4 + b][:]).then_inc(vtok_done, 1)
            for l in range(8):
                act.wait_ge(diff_done, 2 * (l + 1))
                act.activation(e, e, ACT.Exp).then_inc(e_done, 1)
            for b in range(2):
                act.wait_ge(off_ready, b + 1)
                act.copy(flat(k.t(work + 16 + 2 * b, 2)), k.ps[4 + b][:]).then_inc(off_done, 1)
            for h in range(H):
                act.wait_ge(o_ready, h + 1)
                act.copy(k.t(out_slot + h, 1)[:, 0, :], k.ps[h % 4][:, 0:L]).then_inc(o_done, 1)

        @block.vector
        def _(dve):
            dve.wait_ge(masks_in, 16)

            def mask(n):
                for b in range(4):
                    dve.wait_ge(scored, 4 * n + b + 1)
                    if n == 0:
                        dve.tensor_tensor(v4(diag[:, b, :]), v4(k.ps[b][:]), level_mask(-1), ALU.mult).then_inc(masked, 1)
                        continue
                    i = 4 * (n - 1) + b
                    if i >= 2:
                        dve.wait_ge(summed, i - 1)
                    dve.tensor_tensor(v4(tmp[b % 2]), v4(k.ps[b][:]), level_mask(n - 1), ALU.mult).then_inc(masked, 1)

            for l in range(8):
                half = 1 << l
                parts = lambda ap: ap.rearrange("p (n b w) -> p n b w", b=2, w=half)
                left, right = (lambda ap: parts(ap)[:, :, 0, :]), (lambda ap: parts(ap)[:, :, 1, :])
                mid = left(total)[:, :, half - 1:half].broadcast_to([P, H * L // 2 // half, half])
                if l:
                    dve.wait_ge(qk_done, 2 * l)
                dve.tensor_tensor(left(e), mid, left(total), ALU.subtract).then_inc(diff_done, 1)
                dve.tensor_tensor(right(e), right(total), mid, ALU.subtract).then_inc(diff_done, 1)
                mask(l)
                dve.wait_ge(e_done, l + 1)
                dve.tensor_tensor(left(qk), left(key), left(e), ALU.mult).then_inc(qk_done, 1)
                dve.tensor_tensor(right(qk), right(q), right(e), ALU.mult).then_inc(qk_done, 1)

        @block.gpsimd
        def _(pool):
            for i in range(28):
                pool.wait_ge(masked, 4 + i + 1)
                if i >= 4:
                    pool.wait_ge(summed, i - 3)
                pool.tensor_tensor(diag[:, i % 4, :], diag[:, i % 4, :], tmp[i % 2], ALU.add).then_inc(summed, 1)


def causal_conv(k, name, src_slot, dst_slot, tiles, taps, bias, silu):
    W = 4
    with ExitStack() as stage:
        step, activated = (k.sem(stage, f"{name}_{n}") for n in ("step", "activated"))
        block = stage.enter_context(k.nc.Block())

        @block.vector
        def _(dve):
            for g in range(0, tiles, 4):
                for n in range(W):
                    s = n
                    for b in range(4):
                        j = g + b
                        src, dst = k.t(src_slot + j, 1)[:, 0, :], k.t(dst_slot + j, 1)[:, 0, :]
                        w = taps[:, (W - 1 - s) * tiles + j:(W - 1 - s) * tiles + j + 1]
                        if n == 0:
                            ins = dve.tensor_scalar(dst, src, w, bias[:, j:j + 1], ALU.mult, ALU.add)
                        else:
                            dve.wait_ge(step, g * W + 4 * (n - 1) + b + 1)
                            ins = dve.scalar_tensor_tensor(out=dst[:, s:L], in0=src[:, 0:L - s], scalar=w,
                                                           in1=dst[:, s:L], op0=ALU.mult, op1=ALU.add)
                        ins.then_inc(step, 1)

        if silu:
            @block.scalar
            def _(act):
                for g in range(0, tiles, 4):
                    act.wait_ge(step, (g + 4) * W)
                    act.activation(k.t(dst_slot + g, 4), k.t(dst_slot + g, 4), ACT.Silu).then_inc(activated, 1)


def rglru(k, x_slot, z_slot, out_slot, work):
    nc = k.nc
    H = 8
    wa, wx = flat(k.t(work, 4)), flat(k.t(work + 4, 4))
    r, ig, th, a = (flat(k.t(work + 8 + 8 * m, 8)) for m in range(4))
    x, z, out = flat(k.t(x_slot, 8)), flat(k.t(z_slot, 8)), flat(k.t(out_slot, 8))
    s1, s2, s3 = (k.t(199, 1)[:, 0, 8 * m:8 * m + 8] for m in range(3))
    with ExitStack() as stage:
        sem = lambda s: k.sem(stage, f"rglru_{s}")
        w_in, gated, a_small, v_small, sig, act_done, dve_step = (sem(s) for s in (
            "weights_in", "gated", "act_small", "dve_small", "sigmoids", "activations", "dve_step"))
        block = stage.enter_context(nc.Block())

        @block.sync
        def _(sp):
            sp.dma_start(wa, k.i["rg_wa"]).then_inc(w_in, 16)
            sp.dma_start(wx, k.i["rg_wx"]).then_inc(w_in, 16)

        @block.tensor
        def _(pe):
            pe.wait_ge(w_in, 32)
            for h in range(H):
                if h >= 4:
                    pe.wait_ge(sig, 2 * (h - 3))
                for m, w in enumerate((wa, wx)):
                    mm = pe.matmul(k.ps[2 * (h % 4) + m][:, 0:L], w[:, h * P:(h + 1) * P], x[:, h * L:(h + 1) * L],
                                   start=True, stop=True)
                mm.then_inc(gated, 1)

        @block.scalar
        def _(act):
            act.activation(s1, k.col("lam"), ACT.Abs).then_inc(a_small, 1)
            act.wait_ge(a_small, 1)
            act.activation(s1, s1, ACT.Exp, scale=-1.0).then_inc(a_small, 1)
            act.wait_ge(a_small, 2)
            act.activation(s1, s1, ACT.Ln, bias=1.0).then_inc(a_small, 1)
            for h in range(H):
                act.wait_ge(gated, h + 1)
                for m, (dst, b) in enumerate(((r, "ba"), (ig, "bx"))):
                    act.activation(dst[:, h * L:(h + 1) * L], k.ps[2 * (h % 4) + m][:, 0:L], ACT.Sigmoid,
                                   bias=k.col(b)[:, h:h + 1]).then_inc(sig, 1)
            act.wait_ge(v_small, 3)
            act.wait_ge(sig, 2 * H)
            for h in range(H):
                c = slice(h * L, (h + 1) * L)
                act.activation(th[:, c], r[:, c], ACT.Tanh, scale=s2[:, h:h + 1]).then_inc(act_done, 1)
                act.activation(a[:, c], r[:, c], ACT.Exp, scale=s3[:, h:h + 1]).then_inc(act_done, 1)
            act.wait_ge(dve_step, 3)
            act.activation(th, th, ACT.Sqrt, scale=2.0).then_inc(act_done, 1)

        @block.vector
        def _(dve):
            dve.wait_ge(a_small, 3)
            dve.tensor_scalar(s2, k.col("lam"), -1.0, 0.0, ALU.mult, ALU.max).then_inc(v_small, 1)
            dve.wait_ge(v_small, 1)
            dve.tensor_tensor(s1, s1, s2, ALU.add).then_inc(v_small, 1)
            dve.wait_ge(v_small, 2)
            dve.tensor_scalar(s2, s1, 8.0, None, ALU.mult)
            dve.tensor_scalar(s3, s1, -8.0, None, ALU.mult).then_inc(v_small, 1)
            dve.wait_ge(act_done, 2 * H)
            dve.tensor_scalar(r, th, 1.0, None, ALU.add).then_inc(dve_step, 1)
            dve.wait_ge(dve_step, 1)
            dve.reciprocal(r, r).then_inc(dve_step, 1)
            dve.wait_ge(dve_step, 2)
            dve.tensor_tensor(th, th, r, ALU.mult).then_inc(dve_step, 1)
            dve.tensor_tensor(ig, ig, x, ALU.mult).then_inc(dve_step, 1)
            dve.wait_ge(act_done, 2 * H + 1)
            dve.wait_ge(dve_step, 4)
            dve.tensor_tensor(ig, ig, th, ALU.mult).then_inc(dve_step, 1)
            dve.wait_ge(dve_step, 5)
            for h in range(H):
                c = slice(h * L, (h + 1) * L)
                dve.tensor_tensor_scan(th[:, c], a[:, c], ig[:, c], 0.0, ALU.mult, ALU.add).then_inc(dve_step, 1)
            dve.wait_ge(dve_step, 13)
            dve.tensor_tensor(out, th, z, ALU.mult).then_inc(dve_step, 1)


def ssd(k, x_slot, z_slot, out_slot, work):
    nc = k.nc
    H, G = 16, 2
    xs = lambda j: k.t(x_slot + j, 1)[:, 0, :]
    xdt = flat(k.t(work, 8)).rearrange("p (t h c) -> p t h c", t=2, h=H)
    cbm = flat(k.t(work + 8, 3)).rearrange("p (g c) -> p g c", g=G)
    lm = [flat(k.t(work + 11 + 2 * b, 2))[:, 0:384] for b in range(2)]
    dt, da, t1 = (k.t(work + 16 + m, 1)[0:H, 0, :] for m in range(3))
    small = flat(k.t(work + 19, 1))
    dtok, datok, ccol = (small[:, 32 * m:32 * m + 32].rearrange("p (t h) -> p t h", t=2) for m in range(3))
    nega = small[0:H, 96:97]
    incl = flat(k.t(work + 20, 1))[:, 0:P]
    with ExitStack() as stage:
        sem = lambda s: k.sem(stage, f"ssd_{s}")
        w_in, a_step, v_step, dt_turned, da_placed, cum_ready, cb_ready, turned, xdt_done = (sem(s) for s in (
            "incl_in", "act_step", "dve_step", "dt_turned", "da_placed", "cum_ready", "cb_ready",
            "turned", "xdt_done"))
        cb_done, row_ready, diff_done, exp_done, lm_done, y_ready, y_done, gated = (sem(s) for s in (
            "cb_done", "row_ready", "diff_done", "exp_done", "lm_done", "y_ready", "y_done", "gated"))
        block = stage.enter_context(nc.Block())

        @block.sync
        def _(sp):
            sp.dma_start(incl, k.i["cst"][:, 256 + 14 * P:256 + 15 * P]).then_inc(w_in, 16)

        @block.tensor
        def _(pe):
            pe.wait_ge(w_in, 16)
            for g in range(G):
                B, C = xs(8 + g), xs(10 + g)
                pe.matmul(k.ps[2 + g][:, 0:L], B[:, 0:P], C, start=True, stop=True)
                mm = pe.matmul(k.ps[2 + g][:, L:384], B[:, P:L], C[:, P:L], start=True, stop=True)
            mm.then_inc(cb_ready, 1)
            for b in range(4):
                tt, q = b // 2, b % 2
                for m in range(4):
                    mm = pe.transpose(k.ps[4 + b][:, m * P:(m + 1) * P], xs(4 * q + m)[:, tt * P:(tt + 1) * P], k.ident[:])
                mm.then_inc(turned, 1)
            pe.wait_ge(v_step, 5)
            for tt in range(2):
                pe.transpose(k.ps[1][:, 16 * tt:16 * tt + 16], dt[:, tt * P:(tt + 1) * P], k.ident[0:H, 0:H])
                mm = pe.transpose(k.ps[1][:, 32 + 16 * tt:48 + 16 * tt], da[:, tt * P:(tt + 1) * P], k.ident[0:H, 0:H])
            mm.then_inc(dt_turned, 1)
            pe.wait_ge(da_placed, 1)
            pe.matmul(k.ps[0][:, 0:H], incl, datok[:, 0, :], start=True, stop=True)
            pe.matmul(k.ps[0][:, H:2 * H], k.ones, datok[:, 0, :], start=True, stop=False)
            pe.matmul(k.ps[0][:, H:2 * H], incl, datok[:, 1, :], start=False, stop=True).then_inc(cum_ready, 1)
            pe.wait_ge(cb_done, 2)
            pe.wait_ge(v_step, 6)
            pe.wait_ge(xdt_done, 4)
            for h in range(H + 1):
                if h < H:
                    b = k.ps[h % 2]
                    if h >= 2:
                        pe.wait_ge(diff_done, h - 1)
                    d = [datok[:, tt, h:h + 1].broadcast_to([P, P]) for tt in range(2)]
                    pe.matmul(b[:, 0:P], d[0], incl, start=True, stop=True)
                    pe.matmul(b[:, P:L], d[0], k.ones, start=True, stop=False)
                    pe.matmul(b[:, P:L], d[1], incl, start=False, stop=True).then_inc(row_ready, 1)
                if h > 0:
                    g = h - 1
                    y = k.ps[4 + g % 4]
                    pe.wait_ge(lm_done, g + 1)
                    if g >= 4:
                        pe.wait_ge(y_done, g - 3)
                    pair = lambda tt: xdt[:, tt, 2 * (g // 2):2 * (g // 2) + 2, :].rearrange("p h c -> p (h c)")
                    pe.matmul(y[:, 0:L], pair(0), lm[g % 2][:, 0:L], start=True, stop=False, skip_group_check=True)
                    pe.matmul(y[:, P:L], pair(1), lm[g % 2][:, L:384], start=False, stop=True,
                              skip_group_check=True).then_inc(y_ready, 1)

        @block.scalar
        def _(act):
            act.activation(nega, k.col("ssd_alog")[0:H, :], ACT.Exp).then_inc(a_step, 1)
            act.wait_ge(v_step, 1)
            act.activation(t1, dt, ACT.Abs).then_inc(a_step, 1)
            act.wait_ge(a_step, 2)
            act.activation(t1, t1, ACT.Exp, scale=-1.0).then_inc(a_step, 1)
            act.wait_ge(a_step, 3)
            act.activation(t1, t1, ACT.Ln, bias=1.0).then_inc(a_step, 1)
            for h in range(H):
                act.wait_ge(diff_done, h + 1)
                act.activation(lm[h % 2], lm[h % 2], ACT.Exp).then_inc(exp_done, 1)

        @block.vector
        def _(dve):
            dve.tensor_scalar(dt, k.dt_raw[0:H, :], k.col("ssd_dtb")[0:H, :], None, ALU.add).then_inc(v_step, 1)
            dve.wait_ge(a_step, 1)
            dve.tensor_scalar(nega, nega, -1.0, None, ALU.mult).then_inc(v_step, 1)
            dve.wait_ge(a_step, 4)
            dve.wait_ge(v_step, 1)
            dve.scalar_tensor_tensor(out=dt, in0=dt, scalar=0.0, in1=t1, op0=ALU.max, op1=ALU.add).then_inc(v_step, 1)
            dve.wait_ge(v_step, 3)
            dve.tensor_scalar(da, dt, nega, None, ALU.mult).then_inc(v_step, 1)
            dve.wait_ge(v_step, 4)
            dve.wait_ge(w_in, 16)
            dve.wait_ge(cb_ready, 1)
            m3 = incl
            for g in range(G):
                src, dst = k.ps[2 + g], cbm[:, g, :]
                dve.tensor_tensor(dst[:, 0:P], src[:, 0:P], m3, ALU.mult)
                dve.tensor_copy(dst[:, P:L], src[:, P:L])
                dve.tensor_tensor(dst[:, L:384], src[:, L:384], m3, ALU.mult).then_inc(cb_done, 1)
            dve.wait_ge(cb_done, 2)
            dve.nop().then_inc(v_step, 1)
            dve.wait_ge(dt_turned, 1)
            dve.tensor_copy(small[:, 0:64], k.ps[1][:, 0:64]).then_inc(da_placed, 1)
            dve.wait_ge(da_placed, 1)
            for b in range(4):
                tt, q = b // 2, b % 2
                dve.wait_ge(turned, b + 1)
                dve.tensor_tensor(xdt[:, tt, 8 * q:8 * q + 8, :], k.ps[4 + b][:].rearrange("p (h c) -> p h c", c=64),
                                  dtok[:, tt, 8 * q:8 * q + 8].unsqueeze(2).broadcast_to([P, 8, 64]),
                                  ALU.mult).then_inc(xdt_done, 1)
            dve.wait_ge(cum_ready, 1)
            dve.tensor_copy(small[:, 64:96], k.ps[0][:, 0:32]).then_inc(v_step, 1)
            dve.wait_ge(v_step, 6)
            for h in range(H + 2):
                if h < H:
                    dve.wait_ge(row_ready, h + 1)
                    if h >= 2:
                        dve.wait_ge(y_ready, h - 1)
                    dve.tensor_scalar(lm[h % 2][:, 0:L], k.ps[h % 2][:, 0:L], ccol[:, 0, h:h + 1], 0.0,
                                      ALU.subtract, ALU.min)
                    dve.tensor_scalar(lm[h % 2][:, L:384], k.ps[h % 2][:, P:L], ccol[:, 1, h:h + 1], 0.0,
                                      ALU.subtract, ALU.min).then_inc(diff_done, 1)
                if 0 <= h - 1 < H:
                    g = h - 1
                    dve.wait_ge(exp_done, g + 1)
                    dve.tensor_tensor(lm[g % 2], lm[g % 2], cbm[:, g // 8, :], ALU.mult).then_inc(lm_done, 1)
                if 0 <= h - 2:
                    g = h - 2
                    rows = slice(64 * (g % 2), 64 * (g % 2) + 64)
                    dve.wait_ge(y_ready, g + 1)
                    dve.scalar_tensor_tensor(out=k.t(out_slot + g // 2, 1)[rows, 0, :], in0=xs(g // 2)[rows, :],
                                             scalar=k.col("ssd_d")[rows, g // 2:g // 2 + 1],
                                             in1=k.ps[4 + g % 4][rows, 0:L], op0=ALU.mult, op1=ALU.add).then_inc(y_done, 1)
            dve.wait_ge(y_done, H)
            dve.tensor_tensor(k.t(out_slot, 8), k.t(out_slot, 8), k.t(z_slot, 8), ALU.mult).then_inc(gated, 1)


def program(nc, inputs, out):
    with ExitStack() as ctx:
        k = Core(nc, ctx, inputs)
        i = inputs

        def one(slot, count):
            return lambda j: k.t(slot, count)[:, bass.ds(j, 1), :].rearrange("p s c -> p (s c)")

        def fixed(slot):
            return lambda kt: k.t(slot + kt, 1)[:, 0, :]

        def rounded(slot):
            return lambda kt: k.r(slot + kt, 1)[:, 0, :]

        x1_saved = nc.dram_tensor("x1_saved", (P, KT, L), F32).ap()
        x2_saved = nc.dram_tensor("x2_saved", (P, KT, L), F32).ap()

        def keep(slot, count, func=ACT.Copy):
            def evac(act, j, ps):
                return act.activation(one(slot, count)(j), ps, func)
            return evac

        w_in = i["w_in"]
        prologue(k, w_in)
        rms_norm(k, "norm1", lambda t: k.x_ctx(slice(0, 2 * L))[:, t, :],
                 lambda t, a: k.t(32 + t + (16 if a else 0), 1)[:, 0, :],
                 lambda b: k.t(96 + 2 * b, 2).rearrange("p s c -> p (s c)"), 2 * L,
                 [(0, L, k.gain1[:, 0:16], k.mod_x[:, 0:16]), (L, 2 * L, k.gain1[:, 16:32], k.mod_c[:, 0:16])],
                 wait_tokens=True)

        def load_taps(sp):
            sp.dma_start(k.t(192, 2).rearrange("p s c -> p (s c)")[:, 0:KT * WIDTH], i["taps31"]).then_inc(k.taps_in, 16)
            sp.dma_start(k.t(194, 1)[:, 0, 0:48 * SHORT], i["taps5"]).then_inc(k.taps_in, 16)

        split(k, "split_h", 32, 160, 176)
        linear3(k, "gate", w_in[0:16], 16, rounded(160), rounded(176), "scalar", keep(64, 16, ACT.Sigmoid),
                w_in[16:18], side={"sync": load_taps})
        linear3(k, "glu", w_in[16:32], 16, rounded(160), rounded(176), "vector",
                lambda dve, j, ps: dve.tensor_tensor(one(64, 16)(j), ps, one(64, 16)(j), ALU.mult),
                following=w_in[32:36])
        linear(k, "kv", w_in[32:64], 32, k.hx, 2 * L, "scalar",
               lambda act, j, ps: act.copy(k.t(80, 64)[:, bass.ds(j * 2, 2), :].rearrange("p s c -> p (s c)"), ps),
               w_in[64:68], side=grid_conv_side(k))
        linear(k, "q", w_in[64:80], 16, fixed(32), L, "scalar", keep(160, 16), i["w_conv_out"])
        layer_norm_silu(k, 144)
        linear(k, "conv_out", i["w_conv_out"], 16, fixed(144), L, "scalar", keep(64, 16),
               side=short_conv_side(k), following3=w_in[80:82])
        delta_gates(k)
        tile2 = lambda slot, n: lambda j: k.t(slot, n)[:, bass.ds(j * 2, 2), :].rearrange("p s c -> p (s c)")
        channel_norm(k, "knorm", tile2(80, 32), 16, 1, 2 * L, 1.0, k.eps[:, 0:1], 176, before=ACT.Silu)
        channel_norm(k, "qnorm", one(160, 16), 16, 1, L, float(P), k.eps[:, 1:2], 176, before=ACT.Silu)
        with ExitStack() as stage:
            v_done = k.sem(stage, "v_done")
            block = stage.enter_context(nc.Block())

            @block.scalar
            def _(act):
                for q in range(8):
                    act.activation(k.t(112 + 4 * q, 4), k.t(112 + 4 * q, 4), ACT.Silu).then_inc(v_done, 1)
        gated_delta(k)

        split(k, "split_h2", 32, 48, 32)
        linear3(k, "br_conv", w_in[80:96], 16, rounded(48), rounded(32), "scalar", keep(144, 16, ACT.Sigmoid), w_in[96:98])
        elementwise(k, "gate_conv", [lambda dve, q=q: dve.tensor_tensor(
            k.t(64 + 4 * q, 4), k.t(64 + 4 * q, 4), k.t(144 + 4 * q, 4), ALU.mult) for q in range(4)])
        linear3(k, "z", w_in[96:112], 16, rounded(48), rounded(32), "scalar", keep(176, 16, ACT.Silu), w_in[112:114])
        linear3(k, "br_dn", w_in[112:128], 16, rounded(48), rounded(32), "scalar", keep(144, 16, ACT.Sigmoid),
                i["w_dn_out"])
        o, z, br = one(160, 16), one(176, 16), one(144, 16)
        channel_norm(k, "onorm", o, 16, 1, L, 1.0 / P, k.eps[:, 0:1], 48,
                     after=lambda dve, j: dve.scalar_tensor_tensor(
                         out=o(j), in0=o(j), scalar=k.col("dn_g"), in1=z(j), op0=ALU.mult, op1=ALU.mult))

        def load_x(sp):
            sp.dma_start(k.t(32, 16), i["x"]).then_inc(k.tokens_in, 16)

        split(k, "split_o", 160, 176, 160)
        linear3(k, "dn_out", i["w_dn_out"], 16, rounded(176), rounded(160), "vector",
               lambda dve, j, ps: dve.tensor_tensor(br(j), ps, br(j), ALU.mult), i["w_out"], side={"sync": load_x})
        elementwise(k, "merge", [lambda dve, q=q: dve.tensor_tensor(k.t(64 + 4 * q, 4), k.t(64 + 4 * q, 4),
                                                                    k.t(144 + 4 * q, 4), ALU.add) for q in range(4)])
        x1 = one(32, 16)

        def add_mixer(dve, j, ps):
            dve.wait_ge(k.tokens_in, 48)
            return dve.scalar_tensor_tensor(out=x1(j), in0=ps, scalar=k.mod_x[:, bass.ds(j + 32, 1)], in1=x1(j),
                                            op0=ALU.mult, op1=ALU.add)

        split(k, "split_y", 64, 80, 64)
        linear3(k, "w_out", i["w_out"], 16, rounded(80), rounded(64), "vector", add_mixer, i["peer_w_q"])
        rms_norm(k, "norm2", fixed(32), lambda t, a: fixed(48)(t), lambda b: k.t(80 + b, 1)[:, 0, :], L,
                 [(0, L, k.gain2, k.mod_x[:, 48:64])])
        u = i["peer_u"]
        save(k, "x1", 32, x1_saved)
        split(k, "split_t", 48, 80, 96)
        linear3(k, "peer_q", i["peer_w_q"], 16, rounded(80), rounded(96), "scalar", keep(64, 16), following=u[0:4])
        peer_scores(k, 64, 80, 176)
        FIRST = 24
        linear(k, "experts", u[0:FIRST], FIRST, fixed(48), L, "scalar", keep(64, FIRST, ACT.Gelu_apprx_tanh),
               side=peer_select_side(k, 176), following3=u[FIRST:FIRST + 2])
        v = i["peer_v"]
        split(k, "split_t2", 48, 32, 48)
        linear3(k, "experts2", u[FIRST:P], P - FIRST, rounded(32), rounded(48), "scalar",
                keep(64 + FIRST, P - FIRST, ACT.Gelu_apprx_tanh), v[0:2])
        peer_weights(k, 64)
        w2 = i["w_in_2"]
        expert_output(k, v, 64, 32, k.mod_x[:, 80:96], x1_saved, w2[0:2])
        rms_norm(k, "final1", fixed(32), lambda t, a: fixed(32)(t), lambda b: k.t(80 + b, 1)[:, 0, :], L,
                 [(0, L, k.col("final_g"), None)])
        rms_norm(k, "norm_2", fixed(32), lambda t, a: fixed(48)(t), lambda b: k.t(80 + b, 1)[:, 0, :], L,
                 [(0, L, k.col("norm_w"), None)])
        save(k, "x2", 32, x2_saved)
        dt_product(k, 48)
        split(k, "split_h3", 48, 32, 48)

        linear3(k, "in2", w2[0:44], 44, rounded(32), rounded(48), "scalar", keep(64, 44), w2[44:46])
        linear3(k, "in2z", w2[44:68], 24, rounded(32), rounded(48), "scalar", keep(108, 24, ACT.Silu), w2[68:70])
        hgrn_decays(k, 64, 132, 140, 148)
        hgrn_attention(k, 72, 80, 140, 148, 64, 156)
        oa, za, ga = one(64, 8), one(108, 8), k.col("hgrn_g")
        channel_norm(k, "hgrn_norm", oa, 8, 1, L, 1.0 / P, k.eps[:, 0:1], 132,
                     after=lambda dve, j: dve.scalar_tensor_tensor(
                         out=oa(j), in0=oa(j), scalar=k.cols[:, bass.ds(j + COL_AT["hgrn_g"][0], 1)], in1=za(j),
                         op0=ALU.mult, op1=ALU.mult))
        causal_conv(k, "rg_conv", 88, 132, 8, k.col("rg_cw"), k.col("rg_cb"), False)
        rglru(k, 132, 116, 88, 140)
        causal_conv(k, "ssd_conv", 96, 132, 12, k.col("ssd_cw"), k.col("ssd_cb"), True)
        ssd(k, 132, 124, 96, 144)
        oc = one(96, 8)
        channel_norm(k, "ssd_norm", oc, 8, 4, L, 1.0 / 512, k.eps[:, 0:1], 132,
                     after=lambda dve, j: dve.tensor_scalar(
                         oc(j), oc(j), k.cols[:, bass.ds(j + COL_AT["ssd_g"][0], 1)], None, ALU.mult))
        wo2 = i["w_out_2"]
        linear3(k, "gates2", w2[68:116], 48, rounded(32), rounded(48), "scalar", keep(132, 48, ACT.Sigmoid), wo2[0:2])

        def load_x2(sp):
            sp.dma_start(k.t(32, 16), x2_saved).then_inc(k.tokens_in, 16)

        for b, slot in enumerate((64, 88, 96)):
            gate = lambda j, b=b: flat(k.t(132 + 16 * b, 16)[:, bass.ds(j * 2, 2), :])
            split(k, f"split_b{b}", slot, 108 + 8 * b, slot, 8)
            linear3(k, f"out{b}", wo2[8 * b:8 * b + 8], 8, rounded(108 + 8 * b), rounded(slot), "vector",
                    lambda dve, j, ps, gate=gate: dve.tensor_tensor(gate(j), ps, gate(j), ALU.mult),
                    wo2[8 * b + 8:8 * b + 10] if b < 2 else None, pairs=True,
                    side={"sync": load_x2} if b == 0 else None)
        with ExitStack() as stage:
            block = stage.enter_context(nc.Block())

            @block.vector
            def _(dve):
                dve.wait_ge(k.tokens_in, 64)
        for b in range(3):
            elementwise(k, f"add{b}", [lambda dve, q=q, b=b: dve.tensor_tensor(
                k.t(32 + 4 * q, 4), k.t(32 + 4 * q, 4), k.t(132 + 16 * b + 4 * q, 4), ALU.add) for q in range(4)])
        rms_norm(k, "final2", fixed(32), lambda t, a: fixed(32)(t), lambda b: k.t(64 + b, 1)[:, 0, :], L,
                 [(0, L, k.col("final_w"), None)])
        with ExitStack() as stage:
            stored = k.sem(stage, "stored")
            block = stage.enter_context(nc.Block())

            @block.sync
            def _(sp):
                sp.dma_start(out, k.t(32, 16)).then_inc(stored, 16)
                sp.wait_ge(stored, 16)


def _weights(w, kt=KT):
    import numpy as np
    w = np.asarray(w)
    n = w.shape[1] // P
    return np.ascontiguousarray(w.reshape(kt, P, n, P).transpose(2, 1, 0, 3)).reshape(n, P, kt * P)


def _channels(x):
    import numpy as np
    x = np.asarray(x)
    return np.ascontiguousarray(x.T.reshape(-1, P, x.shape[0]).transpose(1, 0, 2))


def _cols(v):
    import numpy as np
    v = np.asarray(v).reshape(-1)
    if v.size % P:
        v = np.concatenate([v, np.zeros(P - v.size % P, v.dtype)])
    return v.reshape(-1, P).T


def _constants():
    import numpy as np
    s, t = np.arange(P)[:, None], np.arange(P)[None, :]
    fwd = [((s >> l) + 1 == (t >> l)) & ((t >> l) % 2 == 1) for l in range(7)]
    parts = [s == t, s == s + 0 * t] + fwd + [m.T for m in fwd] + [s <= t, s >= t, 0 * s + t]
    return np.concatenate([p.astype(np.float32) for p in parts], axis=1)


def layouts(v):
    import numpy as np
    a = {n: np.asarray(x) for n, x in v.items()}
    w_in = a["w_in"][0]
    glu, qkv = w_in[:, 0:4096], w_in[:, 4096:10240]
    z, ab, br = w_in[:, 10240:12288], w_in[:, 12288:12352], w_in[:, 12352:16448]
    q, kk, vv = qkv[:, 0:2048], qkv[:, 2048:4096], qkv[:, 4096:6144]
    cols = {
        "c": a["c"], "c_ctx": a["c_ctx"], "norm1_g": a["norm1_g"], "norm2_g": a["norm2_g"],
        "b_mod": a["b_mod"], "conv_b": a["conv_b"], "ln_g": a["conv_ln_g"], "ln_b": a["conv_ln_b"],
        "dn_g": a["dn_norm_g"], "final_g": a["final_g"], "norm_w": a["norm_w_2"], "hgrn_g": a["hgrn_norm_w_2"],
        "rg_cb": a["rglru_conv_b_2"], "rg_cw": a["rglru_conv_w_2"], "ba": a["rglru_ba_2"],
        "bx": a["rglru_bx_2"], "lam": a["rglru_lambda_2"], "ssd_cw": a["ssd_conv_w_2"],
        "ssd_cb": a["ssd_conv_b_2"], "ssd_g": a["ssd_norm_w_2"], "final_w": a["final_norm_w_2"],
        "ssd_d": np.repeat(a["ssd_d_2"].reshape(-1), 64), "dn_alog": a["dn_a_log"], "dn_dtb": a["dn_dt_bias"],
        "ssd_alog": a["ssd_a_log_2"], "ssd_dtb": a["ssd_dt_bias_2"],
    }
    ab4 = np.concatenate([ab[:, 0:16], ab[:, 32:48], ab[:, 16:32], ab[:, 48:64]], axis=1)
    out = {
        "cols": np.ascontiguousarray(np.concatenate([_cols(cols[n]) for n, _ in COLS], axis=1)),
        "cst": _constants(),
        "x": _channels(a["x"][0]), "ctx": _channels(a["ctx"][0]),
        "w_mod": np.ascontiguousarray(a["w_mod"][0].reshape(4, 4, P, 24, 512).transpose(3, 0, 2, 1, 4)).reshape(96, P, 2048),
        "w_in": _weights(np.concatenate([glu[:, 2048:], glu[:, :2048], kk, vv, q, br[:, :2048], z, br[:, 2048:]], axis=1)),
        "w_ab": np.ascontiguousarray(ab4.reshape(KT, P, 64).transpose(1, 0, 2)).reshape(P, KT * 64),
        "taps31": np.ascontiguousarray(a["conv_w"][0].T.reshape(KT, P, WIDTH).transpose(1, 0, 2)).reshape(P, -1),
        "taps5": np.ascontiguousarray(a["dn_short_w"][0].T.reshape(48, P, SHORT).transpose(1, 0, 2)).reshape(P, -1),
        "w_conv_out": _weights(a["w_conv_out"][0]),
    }
    more_layouts(a, out)
    return out


def more_layouts(a, out):
    import numpy as np
    out["w_dn_out"], out["w_out"] = _weights(a["w_dn_out"][0]), _weights(a["w_out"][0])
    out["peer_w_q"] = _weights(a["peer_w_q"][0])
    keys = [a[n][0].transpose(2, 0, 1).reshape(P, -1) for n in ("peer_key1", "peer_key2")]
    out["peer_keys"] = np.ascontiguousarray(np.concatenate(keys, axis=1))
    out["peer_u"] = _weights(a["peer_u"][0].T)
    out["peer_v"] = a["peer_v"][0].reshape(P, P, D)
    w2 = a["w_in_2"][0]
    q, f, i_, za, bx, bz, cz, xbc, dt, gates = np.split(
        w2, np.cumsum([1024] * 7 + [1536, 16])[:].tolist(), axis=1)
    out["w_in_2"] = _weights(np.concatenate([f, q, i_, bx, xbc, za, bz, cz, gates], axis=1))
    out["w_dt"] = np.ascontiguousarray(dt.reshape(KT, P, 16).transpose(1, 0, 2)).reshape(P, KT * 16)
    out["rg_wa"] = np.ascontiguousarray(a["rglru_wa_2"][0].transpose(1, 0, 2)).reshape(P, 8 * P)
    out["rg_wx"] = np.ascontiguousarray(a["rglru_wx_2"][0].transpose(1, 0, 2)).reshape(P, 8 * P)
    wo = a["w_out_2"][0]
    out["w_out_2"] = np.ascontiguousarray(np.concatenate(
        [_weights(wo[1024 * b:1024 * b + 1024], 8) for b in range(3)]).reshape(24, 2, P, 1024).transpose(0, 2, 1, 3)
    ).reshape(24, P, 2048)


def kernel(**inputs):
    import numpy as np
    import concourse.bacc as bacc
    from concourse.bass_utils import run_bass_kernel_spmd

    arrays = layouts(inputs)
    nc = bacc.Bacc("TRN2", target_bir_lowering=False, num_devices=1)
    aps = {n: nc.dram_tensor(f"in_{n}", a.shape, mybir.dt.from_np(a.dtype), kind="ExternalInput").ap()
           for n, a in arrays.items()}
    out = nc.dram_tensor("out", (P, KT, L), F32, kind="ExternalOutput").ap()
    program(nc, aps, out)
    r = run_bass_kernel_spmd(nc, [{f"in_{n}": a for n, a in arrays.items()}], core_ids=[0])
    y = r.results[0]["out"]
    return np.ascontiguousarray(y.transpose(2, 1, 0)).reshape(1, L, D)
```
